# Optimizing a Trainium2 kernel written in Bass

```python
import math
import jax, jax.numpy as jnp
from jax import lax
import numpy as np

D_MODEL = 2048
BATCH = 1
SEQ = 512
DEPTH = 2

N_MIXERS = 4
MIX_WIDTH = D_MODEL
GROUP_WIDTH = MIX_WIDTH // N_MIXERS
HEAD_DIM = 128
N_HEADS = GROUP_WIDTH // HEAD_DIM
GLA_DK = HEAD_DIM // 2
GLA_DV = HEAD_DIM
GLA_RANK = 16
GLA_GATE_NORM = 16.0
GLA_CHUNK = 64
SWA_KV_HEADS = N_HEADS // 2
SWA_WINDOW = 128
DIFF_DQK = HEAD_DIM // 2
DIFF_BLOCK = 128
GDN_CONV = 4
GDN_CHUNK = 64
NORM_EPS = 1e-6

PROJ_SIZES = (
    N_HEADS * GLA_DK, N_HEADS * GLA_DK, N_HEADS * GLA_DV, GLA_RANK, GROUP_WIDTH,
    N_HEADS * HEAD_DIM, SWA_KV_HEADS * HEAD_DIM, SWA_KV_HEADS * HEAD_DIM, GROUP_WIDTH,
    N_HEADS * 2 * DIFF_DQK, N_HEADS * 2 * DIFF_DQK, N_HEADS * HEAD_DIM, GROUP_WIDTH,
    3 * GROUP_WIDTH, N_HEADS, N_HEADS, GROUP_WIDTH,
)
PROJ_WIDTH = 7192

kernel_name = "hybrid_parallel_heads_gla_swa_diff_gdn"

def rms_norm(x, g):
    xf = x.astype(jnp.float32)
    y = xf * lax.rsqrt(jnp.mean(xf * xf, axis=-1, keepdims=True) + NORM_EPS)
    return (y * g.astype(jnp.float32)).astype(x.dtype)

def l2_norm(x):
    return x * lax.rsqrt(jnp.sum(x * x, axis=-1, keepdims=True) + NORM_EPS)

def alibi_slopes():
    n = 2 * N_HEADS
    s = jnp.asarray(2.0 ** (-8.0 * np.arange(1, n + 1) / n), dtype=jnp.float32)
    return s[0::2], s[1::2]

def causal_conv(x, w):
    K, C = w.shape
    return lax.conv_general_dilated(x, w[:, None, :], window_strides=(1,), padding=[(K - 1, 0)],
                                    dimension_numbers=('NWC', 'WIO', 'NWC'), feature_group_count=C)

def gla_mixer(q, k, v, lr, w_lr2, b_lr2, norm_g):
    dt = q.dtype
    Bn, T, _ = q.shape
    C = GLA_CHUNK
    N = T // C
    g = jax.nn.log_sigmoid((lr @ w_lr2 + b_lr2).astype(jnp.float32)) / GLA_GATE_NORM

    def ch(t, d):
        return t.astype(jnp.float32).reshape(Bn, N, C, N_HEADS, d).transpose(0, 3, 1, 2, 4)

    qc = ch(q, GLA_DK) * GLA_DK ** -0.5
    kc = ch(k, GLA_DK)
    vc = ch(v, GLA_DV)
    b = jnp.cumsum(ch(g, GLA_DK), axis=3)
    b_last = b[:, :, :, -1:, :]
    q_dec = qc * jnp.exp(b)
    k_inv = kc * jnp.exp(-b)
    causal = jnp.tril(jnp.ones((C, C), dtype=bool))
    a = jnp.where(causal, jnp.einsum('bhncd,bhnsd->bhncs', q_dec, k_inv), 0.0)
    o_intra = jnp.einsum('bhncs,bhnsv->bhncv', a, vc)
    u = jnp.einsum('bhncd,bhncv->bhndv', kc * jnp.exp(b_last - b), vc)
    decay = jnp.exp(b_last[:, :, :, 0, :])

    def step(S, inp):
        u_n, d_n = inp
        return d_n[..., None] * S + u_n, S

    S0 = jnp.zeros((Bn, N_HEADS, GLA_DK, GLA_DV), jnp.float32)
    _, S_prev = lax.scan(step, S0, (jnp.moveaxis(u, 2, 0), jnp.moveaxis(decay, 2, 0)))
    o_inter = jnp.einsum('bhncd,nbhdv->bhncv', q_dec, S_prev)
    o = rms_norm(o_intra + o_inter, norm_g)
    return o.transpose(0, 2, 3, 1, 4).reshape(Bn, T, N_HEADS * GLA_DV).astype(dt)

def swa_mixer(q, k, v, q_g, k_g, sinks, slopes):
    dt = q.dtype
    Bn, T, _ = q.shape
    W = SWA_WINDOW
    N = T // W
    G = SWA_KV_HEADS
    R = N_HEADS // G
    d = HEAD_DIM
    q = rms_norm(q.astype(jnp.float32).reshape(Bn, N, W, G, R, d), q_g).transpose(0, 3, 4, 1, 2, 5)
    k = rms_norm(k.astype(jnp.float32).reshape(Bn, N, W, G, d), k_g).transpose(0, 3, 1, 2, 4)
    v = v.astype(jnp.float32).reshape(Bn, N, W, G, d).transpose(0, 3, 1, 2, 4)

    def band(t):
        prev = jnp.pad(t, ((0, 0), (0, 0), (1, 0), (0, 0), (0, 0)))[:, :, :-1]
        return jnp.concatenate([prev, t], axis=3)

    kb, vb = band(k), band(v)
    s = jnp.einsum('bgrnid,bgnjd->bgrnij', q, kb) * d ** -0.5
    i = jnp.arange(W)[:, None]
    j = jnp.arange(2 * W)[None, :]
    dist = i + W - j
    key_pos = jnp.arange(N)[:, None, None] * W + j[None] - W
    valid = (dist >= 0) & (dist < W) & (key_pos >= 0)
    m_h = slopes.reshape(G, R, 1, 1, 1)
    s = jnp.where(valid, s - m_h * dist.astype(jnp.float32), -jnp.inf)
    sink = sinks.astype(jnp.float32).reshape(1, G, R, 1, 1, 1)
    mx = jnp.maximum(jnp.max(s, axis=-1, keepdims=True), sink)
    p = jnp.exp(s - mx)
    p = p / (jnp.sum(p, axis=-1, keepdims=True) + jnp.exp(sink - mx))
    o = jnp.einsum('bgrnij,bgnjd->bgrnid', p, vb)
    return o.transpose(0, 3, 4, 1, 2, 5).reshape(Bn, T, N_HEADS * d).astype(dt)

def diff_mixer(q, k, v, q_g, k_g, lam, subln_g, slopes, lambda_init):
    dt = q.dtype
    Bn, T, _ = q.shape
    H = N_HEADS
    dq = DIFF_DQK
    BLK = DIFF_BLOCK
    N = T // BLK
    q = rms_norm(q.astype(jnp.float32).reshape(Bn, T, H, 2, dq), q_g).transpose(0, 2, 3, 1, 4) * dq ** -0.5
    k = rms_norm(k.astype(jnp.float32).reshape(Bn, T, H, 2, dq), k_g).transpose(0, 2, 3, 1, 4)
    v = v.astype(jnp.float32).reshape(Bn, T, H, HEAD_DIM).transpose(0, 2, 1, 3)
    lam = lam.astype(jnp.float32)
    lam_full = jnp.exp(jnp.sum(lam[0] * lam[1])) - jnp.exp(jnp.sum(lam[2] * lam[3])) + lambda_init
    qb = jnp.moveaxis(q.reshape(Bn, H, 2, N, BLK, dq), 3, 0)
    key_pos = jnp.arange(T)
    m_h = slopes.reshape(1, H, 1, 1, 1)

    def block(args):
        q_blk, n = args
        s = jnp.einsum('bhmid,bhmjd->bhmij', q_blk, k)
        dist = (n * BLK + jnp.arange(BLK))[:, None] - key_pos[None, :]
        s = jnp.where(dist >= 0, s - m_h * dist.astype(jnp.float32), -jnp.inf)
        p = jax.nn.softmax(s, axis=-1)
        w = p[:, :, 0] - lam_full * p[:, :, 1]
        return jnp.einsum('bhij,bhjd->bhid', w, v)

    o = lax.map(block, (qb, jnp.arange(N)))
    o = rms_norm(o, subln_g) * (1.0 - lambda_init)
    o = jnp.moveaxis(o, 0, 2).reshape(Bn, H, T, HEAD_DIM).transpose(0, 2, 1, 3)
    return o.reshape(Bn, T, H * HEAD_DIM).astype(dt)

def gdn_mixer(qkv, beta_raw, a_raw, conv_w, A_log, dt_bias, norm_g):
    dt = qkv.dtype
    Bn, T, _ = qkv.shape
    H = N_HEADS
    d = HEAD_DIM
    C = GDN_CHUNK
    N = T // C
    qkv = jax.nn.silu(causal_conv(qkv, conv_w)).astype(jnp.float32)
    q, k, v = jnp.split(qkv, 3, axis=-1)

    def ch(t):
        return t.reshape(Bn, N, C, H, d).transpose(0, 3, 1, 2, 4)

    qc = l2_norm(ch(q)) * d ** -0.5
    kc = l2_norm(ch(k))
    vc = ch(v)
    beta = jax.nn.sigmoid(beta_raw.astype(jnp.float32)).reshape(Bn, N, C, H).transpose(0, 3, 1, 2)
    g = -jnp.exp(A_log.astype(jnp.float32)) * jax.nn.softplus(a_raw.astype(jnp.float32) + dt_bias.astype(jnp.float32))
    g = g.reshape(Bn, N, C, H).transpose(0, 3, 1, 2)
    dec = jnp.cumsum(g, axis=-1)
    tril = jnp.tril(jnp.ones((C, C), dtype=bool))
    strict = jnp.tril(jnp.ones((C, C), dtype=bool), -1)
    diff = dec[..., :, None] - dec[..., None, :]
    dmask = jnp.where(tril, jnp.exp(jnp.where(tril, diff, 0.0)), 0.0)
    kb = kc * beta[..., None]
    M = jnp.where(strict, jnp.einsum('bhncd,bhnsd->bhncs', kb, kc) * dmask, 0.0)
    eye = jnp.eye(C, dtype=jnp.float32)
    Tm = lax.linalg.triangular_solve(M + eye, jnp.broadcast_to(eye, M.shape), left_side=True,
                                     lower=True, unit_diagonal=True)
    u = jnp.einsum('bhncs,bhnsv->bhncv', Tm, vc * beta[..., None])
    w = jnp.einsum('bhncs,bhnsk->bhnck', Tm, kb * jnp.exp(dec)[..., None])
    qk = jnp.einsum('bhncd,bhnsd->bhncs', qc, kc) * dmask
    q_dec = qc * jnp.exp(dec)[..., None]
    k_end = kc * jnp.exp(dec[..., -1:] - dec)[..., None]
    d_last = jnp.exp(dec[..., -1])

    def step(S, inp):
        u_n, w_n, qd_n, qk_n, ke_n, dl_n = inp
        v_new = u_n - jnp.einsum('bhck,bhkv->bhcv', w_n, S)
        o_n = jnp.einsum('bhck,bhkv->bhcv', qd_n, S) + jnp.einsum('bhcs,bhsv->bhcv', qk_n, v_new)
        S = S * dl_n[..., None, None] + jnp.einsum('bhck,bhcv->bhkv', ke_n, v_new)
        return S, o_n

    S0 = jnp.zeros((Bn, H, d, d), jnp.float32)
    xs = (jnp.moveaxis(u, 2, 0), jnp.moveaxis(w, 2, 0), jnp.moveaxis(q_dec, 2, 0),
          jnp.moveaxis(qk, 2, 0), jnp.moveaxis(k_end, 2, 0), jnp.moveaxis(d_last, 2, 0))
    _, o = lax.scan(step, S0, xs)
    o = rms_norm(o, norm_g)
    return o.transpose(1, 0, 3, 2, 4).reshape(Bn, T, H * d).astype(dt)

def hybrid_layer(x, norm_g, w_in, w_out, gla_w_lr2, gla_b_lr2, gla_norm_g, swa_q_norm_g, swa_k_norm_g,
                 swa_sinks, diff_q_norm_g, diff_k_norm_g, diff_lambda, diff_subln_g, gdn_conv_w, gdn_A_log,
                 gdn_dt_bias, gdn_norm_g, lambda_init):
    h = rms_norm(x, norm_g)
    p = jnp.einsum('btd,dp->btp', h, w_in)
    offs = np.cumsum(np.array(PROJ_SIZES))[:-1].tolist()
    (aq, ak, av, alr, az, bq, bk, bv, bz, cq, ck, cv, cz, dqkv, dbeta, da, dz) = jnp.split(p, offs, axis=-1)
    slopes_b, slopes_c = alibi_slopes()
    ya = gla_mixer(aq, ak, av, alr, gla_w_lr2, gla_b_lr2, gla_norm_g) * jax.nn.silu(az)
    yb = swa_mixer(bq, bk, bv, swa_q_norm_g, swa_k_norm_g, swa_sinks, slopes_b) * jax.nn.silu(bz)
    yc = diff_mixer(cq, ck, cv, diff_q_norm_g, diff_k_norm_g, diff_lambda, diff_subln_g, slopes_c,
                    lambda_init) * jax.nn.silu(cz)
    yd = gdn_mixer(dqkv, dbeta, da, gdn_conv_w, gdn_A_log, gdn_dt_bias, gdn_norm_g) * jax.nn.silu(dz)
    y = jnp.concatenate([ya, yb, yc, yd], axis=-1)
    return x + jnp.einsum('btm,md->btd', y, w_out)

def setup_inputs(seed: int = 0) -> dict:
    key = jax.random.key(seed)
    ks = jax.random.split(key, 20)
    f32 = jnp.float32
    nrm = lambda k, shape: jax.random.normal(k, shape, f32)
    dt = jnp.exp(jax.random.uniform(ks[17], (DEPTH, N_HEADS), f32) * (math.log(0.1) - math.log(0.001)) + math.log(0.001))
    return {
        'x': nrm(ks[0], (BATCH, SEQ, D_MODEL)),
        'norm_g': 1.0 + 0.02 * nrm(ks[1], (DEPTH, D_MODEL)),
        'w_in': nrm(ks[2], (DEPTH, D_MODEL, PROJ_WIDTH)) * D_MODEL ** -0.5,
        'w_out': nrm(ks[3], (DEPTH, MIX_WIDTH, D_MODEL)) * MIX_WIDTH ** -0.5,
        'gla_w_lr2': nrm(ks[4], (DEPTH, GLA_RANK, N_HEADS * GLA_DK)) * GLA_RANK ** -0.5,
        'gla_b_lr2': 0.1 * nrm(ks[5], (DEPTH, N_HEADS * GLA_DK)),
        'gla_norm_g': 1.0 + 0.02 * nrm(ks[6], (DEPTH, GLA_DV)),
        'swa_q_norm_g': 1.0 + 0.02 * nrm(ks[7], (DEPTH, HEAD_DIM)),
        'swa_k_norm_g': 1.0 + 0.02 * nrm(ks[8], (DEPTH, HEAD_DIM)),
        'swa_sinks': nrm(ks[9], (DEPTH, N_HEADS)),
        'diff_q_norm_g': 1.0 + 0.02 * nrm(ks[10], (DEPTH, DIFF_DQK)),
        'diff_k_norm_g': 1.0 + 0.02 * nrm(ks[11], (DEPTH, DIFF_DQK)),
        'diff_lambda': 0.1 * nrm(ks[12], (DEPTH, 4, DIFF_DQK)),
        'diff_subln_g': 1.0 + 0.02 * nrm(ks[13], (DEPTH, HEAD_DIM)),
        'gdn_conv_w': nrm(ks[14], (DEPTH, GDN_CONV, 3 * GROUP_WIDTH)) * GDN_CONV ** -0.5,
        'gdn_A_log': jnp.log(jax.random.uniform(ks[15], (DEPTH, N_HEADS), f32, 1.0, 16.0)),
        'gdn_dt_bias': dt + jnp.log(-jnp.expm1(-dt)),
        'gdn_norm_g': 1.0 + 0.02 * nrm(ks[16], (DEPTH, HEAD_DIM)),
    }

def reference(x, norm_g, w_in, w_out, gla_w_lr2, gla_b_lr2, gla_norm_g, swa_q_norm_g, swa_k_norm_g, swa_sinks,
              diff_q_norm_g, diff_k_norm_g, diff_lambda, diff_subln_g, gdn_conv_w, gdn_A_log, gdn_dt_bias,
              gdn_norm_g):
    for l in range(DEPTH):
        lambda_init = 0.8 - 0.6 * math.exp(-0.3 * l)
        x = hybrid_layer(x, norm_g[l], w_in[l], w_out[l], gla_w_lr2[l], gla_b_lr2[l], gla_norm_g[l],
                         swa_q_norm_g[l], swa_k_norm_g[l], swa_sinks[l], diff_q_norm_g[l], diff_k_norm_g[l],
                         diff_lambda[l], diff_subln_g[l], gdn_conv_w[l], gdn_A_log[l], gdn_dt_bias[l],
                         gdn_norm_g[l], lambda_init)
    return x


_drawn_inputs = setup_inputs


def setup_inputs(seed=0):
    import zlib

    import numpy as np

    out = dict(_drawn_inputs(seed))
    spreads = {}
    factors = {'gla_b_lr2': 3.2,
     'gla_norm_g': 6.782,
     'swa_q_norm_g': 8.0,
     'swa_k_norm_g': 8.0,
     'diff_q_norm_g': 8.0,
     'diff_k_norm_g': 8.0,
     'diff_lambda': 4.35,
     'diff_subln_g': 8.0,
     'gdn_norm_g': 7.168,
     'swa_sinks': 64.0}
    for name, (base, spread) in spreads.items():
        noise = np.random.default_rng([zlib.crc32(name.encode()), seed]).standard_normal(out[name].shape)
        drawn = base * np.exp(spread * noise) if base else spread * noise
        out[name] = __import__('jax').numpy.asarray(drawn.astype(out[name].dtype))
    for name, factor in factors.items():
        out[name] = (out[name] * factor).astype(out[name].dtype)
    return out
```

```python
import math
from contextlib import ExitStack

import concourse.bass as bass
import numpy as np
from concourse import mybir

F32 = mybir.dt.float32
F32R = mybir.dt.float32r
U8 = mybir.dt.uint8
ALU = mybir.AluOpType
ACT = mybir.ActivationFunctionType
AX = mybir.AxisListType

P = 128
DEPTH, SEQ, D_MODEL = 2, 512, 2048
TILES = SEQ // P
KT = D_MODEL // P
GW = 512
HEADS, HD, DK = 4, 128, 64
CH = 64
RANK = 16
EPS = 1e-6
BIG = 3.0e38
SLOPES_B = [2.0 ** -(n + 1) for n in range(0, 2 * HEADS, 2)]
SLOPES_C = [2.0 ** -(n + 1) for n in range(1, 2 * HEADS, 2)]

OFF = dict(aq=0, av=512, alr=1024, az=1040, bq=1552, bkv=2064, bz=2576, cq=3088, ck=3600, cv=4112, cz=4624,
           dq=5136, dk=5648, dv=6160, dbeta=6672, da=6676, dz=6680)
CHUNKS = ["dq", "dk", "dv", "dz", "bz", "az", "aq", "av", "bq", "bkv", "cq", "ck", "cv", "cz"]
OUT_GROUPS = [3, 1, 0, 2]
IN_KTS = len(CHUNKS) * KT
OUT_KTS = TILES * 3 * HEADS
LAST_KTS = TILES * HEADS
LAYER_KTS = IN_KTS + OUT_KTS + LAST_KTS
PAIRS = LAYER_KTS // 2
RAW, RING = 4, 4
NSM = RANK + 2 * HEADS

SLOT = dict(dq=4, dk=5, dv=8, dz=3, bz=4, az=5, aq=6, av=7, bq=8, bkv=9, cq=10, ck=11, cv=12, cz=13)
FIRST_SLOT, SLOTS = 3, 11
CONV = dict(dq=10, dk=11, dv=12)
XSLOT = 6

PC = dict(norm=0, y=16, gq_b=32, gk_b=33, gq_c=34, gk_c=35, conv=36)
NPC = 36 + 12 * 4
PR = dict(sink=0, alog=4, dtb=8, lam=12, linit=12 + 4 * DK, one_less=13 + 4 * DK)
NPR = 14 + 4 * DK
LEVELS = 6


class Steps:

    def __init__(self, sem, steps, before=0):
        self.sem, self.steps, self.before = sem, steps, before
        self.place = {s: i + 1 for i, s in enumerate(steps)}
        assert len(self.place) == len(steps)
        self.given = 0

    def at(self, layer, step):
        return layer * len(self.steps) + (self.before + self.place[step])

    def before_layer(self, layer):
        return layer * len(self.steps) + self.before

    def one(self, step):
        assert self.steps[self.given % len(self.steps)] == step, (self.steps[self.given % len(self.steps)], step)
        self.given += 1
        return 1


def names(fmt, *ranges):
    out = [""]
    for r in ranges:
        out = [f"{a}{'.' if a else ''}{x}" for a in out for x in r]
    return [fmt + x for x in out] if fmt else out


T = range(TILES)
H = range(HEADS)

GDN_PE = "gap nat back kk kq m1 y2 p2 pt2 y3 p3 pt3 y4 p4 pt4 y5 p5 pt5 y6 pt6 w v0 s0 o0 v1 s1 o1".split()
GDN_ACT = "sqq sqk lnr rr vn ex qT qdT kT y2 y3 y4 y5 y6 wT gate sqo lno ro".split()
GDN_DVE = ("ag red qn kn qd kb ke ei es0 es1 es2 es3 mt qk xi xti xt1 x1 x2 xt2 x3 xt3 x4 xt4 x5 xt5 xt6 "
           "g1 g2 g3 v0 s00 s01 s02 s03 v1 s10 s11 s12 s13 redo y0 y1 y2y y3y").split()
GLA_PE = "lrT u cum dec tr a us o".split()
GLA_ACT = "abs e l eb enb er dect qkT gate sqo0 sqo1 lno ro".split()
GLA_DVE = "lr g qd ki ke at0 at1 s00 s01 s10 s11 g1 g2 g3 redo y0 y1 y2 y3".split()
SWA_PE = "tr s0 s1 pt0 pt1 pv".split()
SWA_ACT = "sqq sqk lnr rr qT kT p0 p1 p2 p3 es PT0 gate".split()
SWA_DVE = "red q k b0 b1 b2 b3 mx mxs nm es den rd PT1 g1 g2 g3 y0 y1 y2 y3".split()
PREP_PE = "q k".split()
PREP_ACT = "sqq sqk ln r qT kT".split()
PREP_DVE = "red q k".split()
DIF_PE = [f"{s}{h}" for h in H for s in ("s", "t", "v")]
DIF_PE = ["s0", "s1", "t0", "v0", "s2", "t1", "v1", "s3", "t2", "v2", "t3", "v3"]
DIF_ACT = [x for h in H for x in (f"p{h}0", f"p{h}1", f"wT{h}")] + ["gate", "sqo", "lno", "ro"]
DIF_DVE = [x for h in H for x in (f"b{h}0", f"b{h}1", f"m{h}0", f"m{h}1", f"r{h}", f"c{h}", f"w{h}")] + \
    "g1 g2 g3 os redo y0 y1 y2 y3".split()


def hybrid_trunk(nc, x, wstream, wsmall, pcol, prow, wlr, cf, masks, out):
    ctx = ExitStack()
    with ctx:
        def sb(name, shape, dt=F32):
            return ctx.enter_context(nc.sbuf_tensor(name, shape, dt))

        def sem(name):
            return ctx.enter_context(nc.semaphore(name))

        slots = sb("slots", [P, SLOTS, TILES, GW])
        actT_hi = sb("actT_hi", [P, KT, SEQ], F32R)
        actT_lo = sb("actT_lo", [P, KT, SEQ], F32R)
        w_raw = sb("w_raw", [P, RAW, 2, GW])
        w_hi = sb("w_hi", [P, RING, GW], F32R)
        w_lo = sb("w_lo", [P, RING, GW], F32R)
        ws_raw = sb("ws_raw", [P, KT * NSM])
        ws_hi = sb("ws_hi", [P, KT, NSM], F32R)
        ws_lo = sb("ws_lo", [P, KT, NSM], F32R)
        zeros = sb("zeros", [P, 1])
        general = sb("general", [P, 2, GW])
        cf_sb = sb("cf_sb", [P, cf.shape[1]])
        mask_sb = sb("mask_sb", [P, masks.shape[1]], U8)
        pcol_all = sb("pcol_all", [P, DEPTH, NPC])
        prow_all = sb("prow_all", [P, DEPTH, 12])
        pc = sb("pc", [P, NPC])
        pr = sb("pr", [P, 12])
        neg_lam = sb("neg_lam", [P, DEPTH])
        nlam = sb("nlam", [P, 1])
        wlr_all = sb("wlr_all", [RANK + 1, DEPTH, HEADS * DK])
        wlr_sb = sb("wlr_sb", [RANK + 1, HEADS * DK])
        small = sb("small", [P, TILES, NSM + 1])
        stat = sb("stat", [P, 64])
        beta = sb("beta", [P, TILES, HEADS])
        nbeta = sb("nbeta", [P, TILES, HEADS])
        glog = sb("glog", [P, TILES, HEADS])
        decs = sb("decs", [P, 4, TILES, HEADS])
        eps_t = sb("eps_t", [P, 1])

        def slot(n):
            return slots[:, n - FIRST_SLOT]

        xf = slots[:, XSLOT - FIRST_SLOT:XSLOT - FIRST_SLOT + 4].rearrange("p a b c -> p (a b c)") \
            .rearrange("p (t n) -> p t n", t=TILES)

        def unit(n, k):
            return slot(n)[:, k].rearrange("p (h c) -> p h c", h=HEADS)

        gen = [general[:, i].rearrange("p (h c) -> p h c", h=HEADS) for i in range(2)]

        ident = cf_sb[:, 0:128]
        upto = cf_sb[:, 128:256]
        after = cf_sb[:, 256:384]
        before = cf_sb[:, 384:512]
        half = [cf_sb[:, 512:640], cf_sb[:, 640:768]]
        win = cf_sb[:, 768:1024]
        dist = cf_sb[:, 1024:1024 + 896]
        m_x = [mask_sb[:, 128 * i:128 * i + 128] for i in range(LEVELS)]
        m_xt = [mask_sb[:, 128 * (LEVELS + i):128 * (LEVELS + i) + 128] for i in range(LEVELS)]
        m_upto = mask_sb[:, 128 * 2 * LEVELS:128 * 2 * LEVELS + 128]

        def heads(ap):
            return ap.unsqueeze(1).broadcast_to([P, HEADS, 128])

        def cols(ap, n=128, parts=P):
            return ap.unsqueeze(2).broadcast_to([parts, ap.shape[1], n])

        acc = [ctx.enter_context(nc.psum_tensor(f"acc{i}", [P, GW], F32)) for i in range(4)]
        mix = [ctx.enter_context(nc.psum_tensor(f"mix{i}", [P, GW], F32)) for i in range(4)]
        mh = [m[:, :].rearrange("p (h c) -> p h c", h=HEADS) for m in mix]

        U = dict(S=(unit(8, 0), unit(8, 1)), KB=unit(8, 2), KE=unit(8, 3), VN=unit(9, 0), QDT=unit(9, 1),
                 QK=unit(9, 2), AG=unit(9, 2), MT=unit(9, 3), QD=unit(9, 3), GATE=unit(9, 3),
                 X=unit(13, 0), XT=unit(13, 1), QN=unit(13, 2), QT=unit(13, 2), Y=unit(13, 2),
                 KN=unit(13, 3), KT=unit(13, 3), WT=unit(13, 3), EX=gen[0], VW=gen[0], EI=gen[1], SQO=gen[1])
        U["SQ"] = slot(13)[:, 0:2].rearrange("p a (h c) -> p (a h) c", h=HEADS)
        s12 = slot(12).rearrange("p a b -> p (a b)")
        s13 = slot(13).rearrange("p a b -> p (a b)")
        V = dict(LR=s12[0:RANK + 1, 0:128], T0=s12[:, 128:384], G=s12[:, 384:640], EB=s12[:, 640:896],
                 ENB=s12[:, 896:1152], ER=s12[:, 1152:1408], DECT=s12[:, 1408:1412],
                 QD=s13[:, 0:256], KI=s13[:, 256:512], KE=s13[:, 512:768],
                 QKT=s12[:, 1536:2048], GATE=unit(13, 3), SQO=gen[1], AT=gen[0],
                 S=s13[:, 768:1536].rearrange("p (s p2 c) -> p s p2 c", s=3, p2=2))
        s6 = slot(6).rearrange("p a b -> p (a b)")
        s7 = slot(7).rearrange("p a b -> p (a b)")
        W = dict(SQ=s6[:, 0:768].rearrange("p (g c) -> p g c", c=HD), QT=unit(6, 2), GATE=unit(6, 3),
                 SB=s7[:, 0:1024].rearrange("p (h c) -> p h c", h=HEADS),
                 PT=s7[:, 1024:2048].rearrange("p (h c) -> p h c", h=HEADS))
        RQ = general[:, :, :].rearrange("p a (g c) -> p (a g) c", c=DK)
        f3 = [slot(3)[:, i] for i in range(4)]
        Z = dict(S=((f3[0], f3[1]), (f3[2], f3[3])), WT=(unit(4, 0), unit(4, 1)), OS=unit(4, 2), SQO=unit(4, 3),
                 GATE=unit(5, 0))
        ss, rs = stat[:, 0:16], stat[:, 16:32]
        sa, sb2, sc, sd, se = (stat[:, 32 + 4 * i:36 + 4 * i] for i in range(5))
        cden = stat[:, 52:60]

        consts_in, xin, xcopy = sem("consts_in"), sem("xin"), sem("xcopy")
        lam_in = sem("lam_in")
        raw_in = [sem(f"raw_in{i}") for i in range(RAW)]
        zeros_done = sem("zeros_done")
        dve_passed, pe_passed = sem("dve_passed"), sem("pe_passed")
        raw_used, hi_done, w_ready = sem("raw_used"), sem("hi_done"), sem("w_ready")
        ws_hi_done, ws_ready = sem("ws_hi_done"), sem("ws_ready")
        ws_in = sem("ws_in")
        kt_done = sem("kt_done")
        acc_ready, acc_free = sem("acc_ready"), sem("acc_free")
        xres_in, xout = sem("xres_in"), sem("xout")
        lam_steps = sem("lam_steps")
        lam_act = sem("lam_act")

        N_ACC = len(CHUNKS) + 2 * TILES

        def kt_value(l, kt):
            return l * LAYER_KTS + (RING + kt + 1)

        def acc_free_value(l, q, b):
            return l * (4 * N_ACC) + (4 * q + b + 1)

        def acc_free_after(l, q, b):
            return l * (4 * N_ACC) + (4 * q + b + 5)

        def wait_acc(eng, l, q, b, last_kt):
            if b < 3:
                eng.wait_ge(acc_ready, l * (3 * N_ACC) + (3 * q + b + 1))
            else:
                eng.wait_ge(kt_done, kt_value(l, last_kt))

        def lay(prefix, *parts):
            return [f"{prefix}{p}" for p in parts]

        S_PE = Steps(sem("setup_pe"), [f"hT{k}" for k in range(KT)] + ["small", "dec"] +
                     [f"yT{k}" for k in range(KT)])
        S_ACT = Steps(sem("setup_act"), ["sq0", "sq1", "ln", "r"] + [f"hi{k}" for k in range(KT)] +
                      ["lr", "ba", "eb", "aab", "ea", "la", "A", "decs"] + [f"yhi{k}" for k in range(KT)])
        S_DVE = Steps(sem("setup_dve"), ["pc", "pr", "lam", "wlr", "sq2", "sq3"] + [f"x{t}" for t in T] +
                      [f"lo{k}" for k in range(KT)] +
                      ["b1", "beta", "nbeta", "av", "sp", "glog", "gA", "zero_gdn"] +
                      [f"ylo{k}" for k in range(KT)])
        CONV_DVE = Steps(sem("conv_dve"), [f"{c}{b}{s}" for c in ("dq", "dk", "dv") for b in range(4)
                                           for s in ("t3", "t2", "t1", "t0", "one", "rec", "mul")])
        CONV_ACT = Steps(sem("conv_act"), [f"{c}{b}" for c in ("dq", "dk", "dv") for b in range(4)])
        D_PE = Steps(sem("gdn_pe"), names("", T, GDN_PE))
        D_ACT = Steps(sem("gdn_act"), names("", T, GDN_ACT))
        D_DVE = Steps(sem("gdn_dve"), names("", T, GDN_DVE))
        A_PE = Steps(sem("gla_pe"), names("", T, GLA_PE))
        A_ACT = Steps(sem("gla_act"), names("", T, GLA_ACT))
        A_DVE = Steps(sem("gla_dve"), ["zero_s", "zero_a"] + names("", T, GLA_DVE))
        B_PE = Steps(sem("swa_pe"), names("", T, SWA_PE))
        B_ACT = Steps(sem("swa_act"), names("", T, SWA_ACT))
        B_DVE = Steps(sem("swa_dve"), names("", T, SWA_DVE))
        R_PE = Steps(sem("prep_pe"), names("", T, PREP_PE))
        R_ACT = Steps(sem("prep_act"), names("", T, PREP_ACT))
        R_DVE = Steps(sem("prep_dve"), names("", T, PREP_DVE))
        back = list(reversed(T))
        C_PE = Steps(sem("dif_pe"), names("", back, DIF_PE))
        C_ACT = Steps(sem("dif_act"), names("", back, DIF_ACT))
        C_DVE = Steps(sem("dif_dve"), names("", back, DIF_DVE))

        block = ctx.enter_context(nc.Block())

        @block.sync
        def _(sp):
            for t in T:
                sp.dma_start(xf[:, t], x[t * P:(t + 1) * P, :]).then_inc(xin, 16)
            sp.dma_start(cf_sb[:, :], cf).then_inc(consts_in, 16)
            sp.dma_start(slot(10).rearrange("p a b -> p (a b)")[:, 0:masks.shape[1]], masks).then_inc(consts_in, 16)
            sp.dma_start(pcol_all[:, :, :], pcol.rearrange("l p n -> p l n")).then_inc(consts_in, 16)
            for l in range(DEPTH):
                sp.dma_start(prow_all[:, l], prow[l, 0:12].partition_broadcast(P)).then_inc(consts_in, 16)
                sp.dma_start(slot(4)[:, l, 0:NPR], prow[l].partition_broadcast(P)).then_inc(lam_in, 16)
            sp.dma_start(wlr_all[:, :, :], wlr.rearrange("l r n -> r l n")).then_inc(consts_in, 16)
            with sp.Fori(0, DEPTH) as l:
                sp.wait_ge(ws_ready, l + 1)
                sp.dma_start(ws_raw[:, :], wsmall[bass.ds(l, 1)].rearrange("a p n -> p (a n)")).then_inc(ws_in, 16)
                with sp.Fori(0, PAIRS // RAW) as i:
                    for s in range(RAW):
                        sp.wait_ge(raw_used, l * PAIRS + i * RAW + (s + 1))
                        sp.dma_start(w_raw[:, s].rearrange("p a n -> p (a n)"),
                                     wstream[bass.ds(l * PAIRS + i * RAW + s, 1)].rearrange("a p n -> p (a n)")
                                     ).then_inc(raw_in[s], 16)

        @block.gpsimd
        def _(pool):
            pool.sem_inc(raw_used, RAW)
            pool.sem_inc(ws_ready, 1)
            pool.memset(zeros[:, :], 0.0).then_inc(zeros_done, 1)
            pool.wait_ge(zeros_done, 1)
            pool.dma_start(out[:, :], x[:, :]).then_inc(xcopy, 16)
            with pool.Fori(0, DEPTH) as l:
                pool.wait_ge(ws_in, l * 16 + 16)
                pool.wait_ge(kt_done, l * LAYER_KTS + RING)
                pool.tensor_tensor(ws_hi[:, :, :].rearrange("p a b -> p (a b)"), ws_raw[:, :],
                                   zeros[:, :].broadcast_to([P, KT * NSM]), ALU.add).then_inc(ws_hi_done, 1)
                pool.wait_ge(ws_hi_done, l + 1)
                pool.tensor_tensor(ws_lo[:, :, :].rearrange("p a b -> p (a b)"), ws_raw[:, :],
                                   ws_hi[:, :, :].rearrange("p a b -> p (a b)").bitcast(F32),
                                   ALU.subtract).then_inc(ws_ready, 1)
                with pool.Fori(0, PAIRS // RAW) as i:
                    for s in range(RAW):
                        pool.wait_ge(raw_in[s], l * (16 * PAIRS // RAW) + i * 16 + 16)
                        for k in range(2):
                            n, r = 2 * s + k, (2 * s + k) % RING
                            pool.wait_ge(kt_done, l * LAYER_KTS + i * (2 * RAW) + (n + 1))
                            pool.tensor_tensor(w_hi[:, r], w_raw[:, s, k], zeros[:, :].broadcast_to([P, GW]), ALU.add).then_inc(hi_done, 1)
                            pool.wait_ge(hi_done, l * LAYER_KTS + i * (2 * RAW) + (n + 1))
                            pool.tensor_tensor(w_lo[:, r], w_raw[:, s, k], w_hi[:, r].bitcast(F32),
                                               ALU.subtract).then_inc(w_ready, 1)
                        pool.wait_ge(w_ready, l * LAYER_KTS + i * (2 * RAW) + (2 * s + 2))
                        pool.sem_inc(raw_used, 1)

        @block.tensor
        def _(pe):
            pe.sem_inc(kt_done, RING)

            def plain():
                pe.sem_inc(pe_passed, 1)

            def project(l, q, kt0, kts, act_kt, turned=False, ahead=None, mixer=None, stages=1, skip=0):
                slots_n, given = 2 * (kts - skip), 0
                for k in range(kts):
                    if ahead:
                        ahead(k)
                    r = (kt0 + k) % RING
                    pe.wait_ge(w_ready, l * LAYER_KTS + (kt0 + k + 1))
                    for b in range(4):
                        if k == 0:
                            pe.wait_ge(acc_free, acc_free_value(l, q, b))
                        c = slice(b * P, b * P + P)
                        a = act_kt + k
                        if turned:
                            terms = [(w_hi[:, r, c], actT_hi[:, a]), (w_hi[:, r, c], actT_lo[:, a]),
                                     (w_lo[:, r, c], actT_hi[:, a])]
                        else:
                            terms = [(actT_hi[:, a, c], w_hi[:, r]), (actT_hi[:, a, c], w_lo[:, r]),
                                     (actT_lo[:, a, c], w_hi[:, r])]
                        for i, (lhsT, rhs) in enumerate(terms):
                            last = nc.tensor.matmul(acc[b][:, :], lhsT, rhs, start=(k == 0 and i == 0),
                                                    stop=(k == kts - 1 and i == 2))
                        if b == 3:
                            last.then_inc(kt_done, 1)
                        elif k == kts - 1:
                            last.then_inc(acc_ready, 1)
                        if mixer and b % 2 and k >= skip:
                            n = 2 * (k - skip) + b // 2 + 1
                            while given * slots_n < n * stages and given < stages:
                                next(mixer, None)
                                given += 1
                if mixer:
                    for _ in mixer:
                        pass

            def gdn(l, t):
                cs = slice(t * P, t * P + P)
                q, k, v = (slot(CONV[c]) for c in ("dq", "dk", "dv"))
                QN, KN, QD, KB, KE, VN = U["QN"], U["KN"], U["QD"], U["KB"], U["KE"], U["VN"]
                yield
                if t:
                    pe.wait_ge(D_DVE.sem, D_DVE.at(l, f"{t-1}.y3y"))
                else:
                    pe.wait_ge(S_ACT.sem, S_ACT.at(l, "decs"))
                    pe.wait_ge(CONV_DVE.sem, CONV_DVE.at(l, "dv3mul"))
                pe.wait_ge(D_DVE.sem, D_DVE.at(l, f"{t}.ag"))
                for h in H:
                    last = nc.tensor.matmul(mh[3][:, h], U["AG"][:, h], upto, start=True, stop=True)
                last.then_inc(D_PE.sem, D_PE.one(f"{t}.gap"))
                for i, s in enumerate((q, k, v)):
                    for h in H:
                        last = nc.tensor.transpose(mh[i][:, h], s[:, h, cs], ident)
                last.then_inc(D_PE.sem, D_PE.one(f"{t}.nat"))
                yield
                pe.wait_ge(D_DVE.sem, D_DVE.at(l, f"{t}.qd"))
                pe.wait_ge(D_ACT.sem, D_ACT.at(l, f"{t}.vn"))
                for i, s in enumerate((QN, KN, QD)):
                    for h in H:
                        last = nc.tensor.transpose(mh[i][:, h], s[:, h], ident)
                last.then_inc(D_PE.sem, D_PE.one(f"{t}.back"))
                yield
                pe.wait_ge(D_ACT.sem, D_ACT.at(l, f"{t}.kT"))
                for h in H:
                    last = nc.tensor.matmul(mh[0][:, h], U["KT"][:, h], U["KT"][:, h], start=True, stop=True)
                last.then_inc(D_PE.sem, D_PE.one(f"{t}.kk"))
                for h in H:
                    last = nc.tensor.matmul(mh[1][:, h], U["KT"][:, h], U["QT"][:, h], start=True, stop=True)
                last.then_inc(D_PE.sem, D_PE.one(f"{t}.kq"))
                yield
                pe.wait_ge(D_DVE.sem, D_DVE.at(l, f"{t}.mt"))
                for h in H:
                    last = nc.tensor.transpose(mh[2][:, h], U["MT"][:, h], ident)
                last.then_inc(D_PE.sem, D_PE.one(f"{t}.m1"))
                yield
                for lv in range(2, LEVELS + 1):
                    pe.wait_ge(D_DVE.sem, D_DVE.at(l, f"{t}.x{lv-1}"))
                    for h in H:
                        last = nc.tensor.matmul(mh[3][:, h], U["MT"][:, h], U["X"][:, h], start=True, stop=True)
                    last.then_inc(D_PE.sem, D_PE.one(f"{t}.y{lv}"))
                    yield
                    pe.wait_ge(D_ACT.sem, D_ACT.at(l, f"{t}.y{lv}"))
                    pe.wait_ge(D_DVE.sem, D_DVE.at(l, f"{t}.xt{lv-1}"))
                    if lv < LEVELS:
                        for h in H:
                            last = nc.tensor.matmul(mh[0][:, h], U["XT"][:, h], U["Y"][:, h], start=True, stop=True)
                        last.then_inc(D_PE.sem, D_PE.one(f"{t}.p{lv}"))
                    for h in H:
                        last = nc.tensor.matmul(mh[1][:, h], U["Y"][:, h], U["XT"][:, h], start=True, stop=True)
                    last.then_inc(D_PE.sem, D_PE.one(f"{t}.pt{lv}"))
                    yield
                pe.wait_ge(D_DVE.sem, D_DVE.at(l, f"{t}.xt6"))
                for h in H:
                    last = nc.tensor.matmul(mh[2][:, h], KB[:, h], U["XT"][:, h], start=True, stop=True)
                last.then_inc(D_PE.sem, D_PE.one(f"{t}.w"))
                yield
                for j in range(2):
                    r = slice(CH * j, CH * j + CH)
                    S = U["S"][j]
                    pe.wait_ge(D_ACT.sem, D_ACT.at(l, f"{t}.wT"))
                    if j:
                        pe.wait_ge(D_DVE.sem, D_DVE.at(l, f"{t}.s03"))
                    plain()
                    for h in H:
                        nc.tensor.matmul(mh[3][r, h], U["XT"][r, h, r], VN[r, h], start=True, stop=False)
                        last = nc.tensor.matmul(mh[3][r, h], U["WT"][:, h, r], S[:, h], start=False, stop=True)
                    last.then_inc(D_PE.sem, D_PE.one(f"{t}.v{j}"))
                    yield
                    pe.wait_ge(D_DVE.sem, D_DVE.at(l, f"{t}.v{j}"))
                    for h in H:
                        last = nc.tensor.matmul(mh[j][:, h], KE[r, h], U["VW"][r, h], start=True, stop=True)
                    last.then_inc(D_PE.sem, D_PE.one(f"{t}.s{j}"))
                    for h in H:
                        nc.tensor.matmul(mh[2][r, h], U["QDT"][:, h, r], S[:, h], start=True, stop=False)
                        last = nc.tensor.matmul(mh[2][r, h], U["QK"][r, h, r], U["VW"][r, h], start=False, stop=True)
                    last.then_inc(D_PE.sem, D_PE.one(f"{t}.o{j}"))
                    yield

            def gla(l, t):
                yield
                if t:
                    pe.wait_ge(A_DVE.sem, A_DVE.at(l, f"{t-1}.y3"))
                else:
                    pe.wait_ge(D_DVE.sem, D_DVE.at(l, f"{TILES-1}.y3y"))
                nc.tensor.transpose(mix[0][0:RANK + 1, 0:P], small[:, t, 0:RANK + 1], ident) \
                    .then_inc(A_PE.sem, A_PE.one(f"{t}.lrT"))
                yield
                pe.wait_ge(A_DVE.sem, A_DVE.at(l, f"{t}.lr"))
                nc.tensor.matmul(mix[1][:, 0:256], V["LR"], wlr_sb[:, :],
                                 start=True, stop=True).then_inc(A_PE.sem, A_PE.one(f"{t}.u"))
                yield
                pe.wait_ge(A_DVE.sem, A_DVE.at(l, f"{t}.g"))
                nc.tensor.matmul(mix[0][:, 0:256], upto, V["G"], start=True, stop=True)
                nc.tensor.matmul(mix[0][:, 256:512], after, V["G"], start=True, stop=True) \
                    .then_inc(A_PE.sem, A_PE.one(f"{t}.cum"))
                for p in range(2):
                    for j in range(2):
                        last = nc.tensor.matmul(mix[1][:, 2 * p + j:2 * p + j + 1], V["G"][:, p * P:p * P + P],
                                                half[j][:, 0:1], start=True, stop=True)
                last.then_inc(A_PE.sem, A_PE.one(f"{t}.dec"))
                yield
                pe.wait_ge(A_DVE.sem, A_DVE.at(l, f"{t}.ki"))
                for i, s in enumerate((V["QD"], V["KI"])):
                    for p in range(2):
                        last = nc.tensor.transpose(mix[2][:, 256 * i + P * p:256 * i + P * p + P],
                                                   s[:, p * P:p * P + P], ident)
                last.then_inc(A_PE.sem, A_PE.one(f"{t}.tr"))
                yield
                pe.wait_ge(A_ACT.sem, A_ACT.at(l, f"{t}.qkT"))
                for h in H:
                    b, p = slice(DK * (h % 2), DK * (h % 2) + DK), h // 2
                    last = nc.tensor.matmul(mh[3 - h % 2][:, h], V["QKT"][b, 256 + P * p:256 + P * p + P],
                                            V["QKT"][b, P * p:P * p + P], start=True, stop=True)
                last.then_inc(A_PE.sem, A_PE.one(f"{t}.a"))
                pe.wait_ge(A_DVE.sem, A_DVE.at(l, f"{t}.ke"))
                pe.wait_ge(A_ACT.sem, A_ACT.at(l, f"{t}.dect"))
                plain()
                for h in H:
                    for j in range(2):
                        r = slice(CH * j, CH * j + CH)
                        o = slice(DK * (h % 2), DK * (h % 2) + DK)
                        last = nc.tensor.matmul(mh[j][o, h // 2], V["KE"][r, DK * h:DK * h + DK],
                                                slot(SLOT["av"])[r, t, HD * h:HD * h + HD], start=True, stop=True)
                last.then_inc(A_PE.sem, A_PE.one(f"{t}.us"))
                yield
                pe.wait_ge(A_DVE.sem, A_DVE.at(l, f"{t}.s11"))
                for h in H:
                    b, p = slice(DK * (h % 2), DK * (h % 2) + DK), h // 2
                    o = mh[3 if h % 2 else 1]
                    nc.tensor.matmul(o[:, h], V["AT"][:, h], slot(SLOT["av"])[:, t, HD * h:HD * h + HD],
                                     start=True, stop=False)
                    for j in range(2):
                        r = slice(CH * j, CH * j + CH)
                        last = nc.tensor.matmul(o[r, h], V["QKT"][b, P * p + CH * j:P * p + CH * j + CH],
                                                V["S"][b, (2 * t + j) % 3, p], start=False, stop=True)
                last.then_inc(A_PE.sem, A_PE.one(f"{t}.o"))
                yield

            def swa(l, t):
                q, kv = slot(SLOT["bq"]), slot(SLOT["bkv"])
                yield
                if t % 2:
                    pe.wait_ge(R_ACT.sem, R_ACT.at(l, f"{t-1}.kT"))
                elif t:
                    pe.wait_ge(R_ACT.sem, R_ACT.at(l, f"{t-1}.kT"))
                else:
                    pe.wait_ge(A_DVE.sem, A_DVE.at(l, f"{TILES-1}.y3"))
                if t:
                    pe.wait_ge(B_DVE.sem, B_DVE.at(l, f"{t-1}.y3"))
                pe.wait_ge(B_DVE.sem, B_DVE.at(l, f"{t}.k"))
                for h in H:
                    nc.tensor.transpose(mh[0][:, h], q[:, t, h * HD:h * HD + HD], ident)
                for g in range(2):
                    last = nc.tensor.transpose(mh[1][:, g], kv[:, t, g * HD:g * HD + HD], ident)
                last.then_inc(B_PE.sem, B_PE.one(f"{t}.tr"))
                yield
                pe.wait_ge(B_ACT.sem, B_ACT.at(l, f"{t}.kT"))
                n = min(t, 1) + 1
                for h in H:
                    last = nc.tensor.matmul(mix[2 + h // 2][:, 256 * (h % 2):256 * (h % 2) + P * n], W["QT"][:, h],
                                            kv[:, t + 1 - n:t + 1, (h // 2) * HD:(h // 2) * HD + HD],
                                            start=True, stop=True)
                    if h % 2:
                        last.then_inc(B_PE.sem, B_PE.one(f"{t}.s{h//2}"))
                yield
                yield
                yield
                for i in range(2):
                    pe.wait_ge(B_ACT.sem, B_ACT.at(l, f"{t}.p{2*i+1}"))
                    for h in (2 * i, 2 * i + 1):
                        for m in range(n):
                            last = nc.tensor.transpose(mix[i][:, 256 * (h % 2) + P * m:256 * (h % 2) + P * m + P],
                                                       W["SB"][:, h, P * m:P * m + P], ident)
                    last.then_inc(B_PE.sem, B_PE.one(f"{t}.pt{i}"))
                yield
                pe.wait_ge(B_ACT.sem, B_ACT.at(l, f"{t}.PT0"))
                pe.wait_ge(B_DVE.sem, B_DVE.at(l, f"{t}.PT1"))
                for h in H:
                    for m in range(n):
                        last = nc.tensor.matmul(mh[2][:, h], W["PT"][:, h, P * m:P * m + P],
                                                kv[:, t + 1 - n + m, 256 + (h // 2) * HD:256 + (h // 2) * HD + HD],
                                                start=(m == 0), stop=(m == n - 1))
                last.then_inc(B_PE.sem, B_PE.one(f"{t}.pv"))
                yield

            def prep(l, t):
                pe.wait_ge(R_DVE.sem, R_DVE.at(l, f"{t}.k"))
                pe.wait_ge(B_ACT.sem, B_ACT.at(l, f"{t}.PT0"))
                pe.wait_ge(B_DVE.sem, B_DVE.at(l, f"{t}.PT1"))
                for i, c in enumerate(("cq", "ck")):
                    for h in H:
                        last = nc.tensor.transpose(mh[i][:, h], slot(SLOT[c])[:, t, h * HD:h * HD + HD], ident)
                    last.then_inc(R_PE.sem, R_PE.one(f"{t}.{'qk'[i]}"))
                yield

            def dif(l, t):
                n = t + 1
                qT, kT, v = (slot(SLOT[c]) for c in ("cq", "ck", "cv"))

                def scores(h):
                    if h:
                        pe.wait_ge(C_DVE.sem, C_DVE.at(l, f"{t}.b{h-1}1"))
                    elif t < TILES - 1:
                        pe.wait_ge(C_DVE.sem, C_DVE.at(l, f"{t+1}.b{HEADS-1}1"))
                    else:
                        pe.wait_ge(S_DVE.sem, S_DVE.at(l, f"ylo{3*HEADS-1}"))
                    for m in range(2):
                        r = slice(DK * m, DK * m + DK)
                        last = nc.tensor.matmul(mix[m][:, 0:P * n], qT[r, t, HD * h:HD * h + HD],
                                                kT[r, 0:n, HD * h:HD * h + HD], start=True, stop=True)
                    last.then_inc(C_PE.sem, C_PE.one(f"{t}.s{h}"))

                def turn(h):
                    pe.wait_ge(C_DVE.sem, C_DVE.at(l, f"{t}.w{h}"))
                    if h:
                        pe.wait_ge(C_ACT.sem, C_ACT.at(l, f"{t}.wT{h-1}"))
                    for j in range(n):
                        last = nc.tensor.transpose(mh[2][:, j], Z["S"][h % 2][0][:, P * j:P * j + P], ident)
                    last.then_inc(C_PE.sem, C_PE.one(f"{t}.t{h}"))

                def values(h):
                    pe.wait_ge(C_ACT.sem, C_ACT.at(l, f"{t}.wT{h}"))
                    if h == 0 and t < TILES - 1:
                        pe.wait_ge(C_DVE.sem, C_DVE.at(l, f"{t+1}.os"))
                    for j in range(n):
                        last = nc.tensor.matmul(mh[3][:, h], Z["WT"][h % 2][:, j], v[:, j, HD * h:HD * h + HD],
                                                start=(j == 0), stop=(j == n - 1))
                    last.then_inc(C_PE.sem, C_PE.one(f"{t}.v{h}"))

                scores(0)
                yield
                scores(1)
                yield
                for h in H:
                    turn(h)
                    yield
                    values(h)
                    yield
                    if h + 2 < HEADS:
                        scores(h + 2)
                        yield

            def turn_x(l, k):
                if k >= 4:
                    pe.wait_ge(S_DVE.sem, S_DVE.at(l, f"lo{k-4}"))
                for t in T:
                    last = nc.tensor.transpose(mh[k % 4][:, t], xf[:, t, k * P:k * P + P], ident)
                last.then_inc(S_PE.sem, S_PE.one(f"hT{k}"))

            def turn_y(l, k):
                src = slot(SLOT[("dz", "bz", "az", "cz")[k // 4]])
                if k == 0:
                    pe.wait_ge(B_DVE.sem, B_DVE.at(l, f"{TILES-1}.y3"))
                    pe.wait_ge(R_ACT.sem, R_ACT.at(l, f"{TILES-1}.kT"))
                elif k == 3 * HEADS:
                    pe.wait_ge(C_DVE.sem, C_DVE.at(l, "0.y3"))
                elif k >= 4:
                    pe.wait_ge(S_DVE.sem, S_DVE.at(l, f"ylo{k-4}"))
                for t in T:
                    last = nc.tensor.transpose(mh[k % 4][:, t], src[:, t, (k % 4) * P:(k % 4) * P + P], ident)
                last.then_inc(S_PE.sem, S_PE.one(f"yT{k}"))

            with pe.Fori(0, DEPTH) as l:
                pe.wait_ge(S_DVE.sem, S_DVE.at(l, "x3"))
                for k in range(4):
                    turn_x(l, k)

                def h_ready(k):
                    pe.wait_ge(S_DVE.sem, S_DVE.at(l, f"lo{k}"))
                    if k + 4 < KT:
                        turn_x(l, k + 4)

                project(l, 0, 0, KT, 0, turned=True, ahead=h_ready)
                pe.wait_ge(ws_ready, l + 2)
                for t in T:
                    for k in range(KT):
                        for i, (a, w) in enumerate(((actT_hi, ws_hi), (actT_hi, ws_lo), (actT_lo, ws_hi))):
                            last = nc.tensor.matmul(mix[0][:, 32 * t:32 * t + NSM], a[:, k, t * P:t * P + P],
                                                    w[:, k], start=(k == 0 and i == 0), stop=(k == KT - 1 and i == 2))
                last.then_inc(S_PE.sem, S_PE.one("small"))
                project(l, 1, KT, KT, 0, turned=True)
                pe.wait_ge(S_DVE.sem, S_DVE.at(l, "gA"))
                gl = glog[:, :, :].rearrange("p t h -> p (t h)")
                for i, w in enumerate((upto, after, half[0], half[1])):
                    last = nc.tensor.matmul(mix[3][:, 16 * i:16 * i + 16], w, gl, start=True, stop=True)
                last.then_inc(S_PE.sem, S_PE.one("dec"))
                project(l, 2, 2 * KT, KT, 0, turned=True)
                project(l, 3, 3 * KT, KT, 0)
                for t in T:
                    project(l, 4 + t, (4 + t) * KT, KT, 0, mixer=gdn(l, t), stages=22)
                for t in T:
                    project(l, 8 + t, (8 + t) * KT, KT, 0, mixer=gla(l, t), stages=7)
                for i in range(2):
                    def both(l=l, i=i):
                        for t in (2 * i, 2 * i + 1):
                            yield from swa(l, t)
                            yield from prep(l, t)
                    project(l, 12 + i, (12 + i) * KT, KT, 0, mixer=both(), stages=16)
                for k in range(4):
                    turn_y(l, k)
                for n in T:
                    def y_ready(k, n=n):
                        if n == 0:
                            pe.wait_ge(S_DVE.sem, S_DVE.at(l, f"ylo{k}"))
                            for m in (4 + 2 * k, 5 + 2 * k):
                                if m < 3 * HEADS:
                                    turn_y(l, m)
                    project(l, 14 + n, IN_KTS + 12 * n, 12, 0, ahead=y_ready, mixer=dif(l, TILES - 1 - n),
                            stages=12, skip=(4 if n == 0 else 0))
                for k in range(12, 16):
                    turn_y(l, k)
                for n in T:
                    def c_ready(k, n=n):
                        if n == 0:
                            pe.wait_ge(S_DVE.sem, S_DVE.at(l, f"ylo{12+k}"))
                    project(l, 18 + n, IN_KTS + OUT_KTS + 4 * n, 4, 12, ahead=c_ready)

        @block.scalar
        def _(act):
            act.sem_inc(acc_free, 4)
            act.sem_inc(xout, 1)

            def take_out(l, c):
                q = CHUNKS.index(c)
                for b in range(4):
                    wait_acc(act, l, q, b, q * KT + KT - 1)
                    nc.scalar.activation(slot(SLOT[c])[:, b], acc[b][:, :], ACT.Copy).then_inc(acc_free, 1)

            def rms(l, St, t, ln, r, src, dst, scale, ready):
                ready()
                nc.scalar.activation(dst, src, ACT.Ln, bias=eps_t[:, :], scale=scale).then_inc(St.sem, St.one(ln))
                act.wait_ge(St.sem, St.at(l, ln))
                nc.scalar.activation(dst, dst, ACT.Exp, scale=-0.5).then_inc(St.sem, St.one(r))

            act.wait_ge(lam_steps, 2 * DEPTH)
            nc.scalar.activation(stat[:, 32:32 + 2 * DEPTH], stat[:, 0:2 * DEPTH], ACT.Exp).then_inc(lam_act, 1)

            with act.Fori(0, DEPTH) as l:
                act.wait_ge(xin, 16 * TILES)
                act.wait_ge(acc_free, l * (4 * N_ACC) + 4)
                act.wait_ge(S_DVE.sem, S_DVE.at(l, "pc"))
                for t in range(2):
                    nc.scalar.activation(slot(13).rearrange("p a b -> p (a b)") if t else
                                         slot(5).rearrange("p a b -> p (a b)"), xf[:, t], ACT.Square,
                                         accum_out=ss[:, t:t + 1]).then_inc(S_ACT.sem, S_ACT.one(f"sq{t}"))
                act.wait_ge(S_ACT.sem, S_ACT.at(l, "sq1"))
                act.wait_ge(S_DVE.sem, S_DVE.at(l, "sq3"))
                nc.scalar.activation(rs[:, 0:4], ss[:, 0:4], ACT.Ln, bias=eps_t[:, :],
                                     scale=1.0 / D_MODEL).then_inc(S_ACT.sem, S_ACT.one("ln"))
                act.wait_ge(S_ACT.sem, S_ACT.at(l, "ln"))
                nc.scalar.activation(rs[:, 0:4], rs[:, 0:4], ACT.Exp, scale=-0.5).then_inc(S_ACT.sem, S_ACT.one("r"))
                for k in range(KT):
                    act.wait_ge(S_PE.sem, S_PE.at(l, f"hT{k}"))
                    nc.scalar.activation(actT_hi[:, k], mix[k % 4][:, :], ACT.Copy,
                                         scale=pc[:, PC["norm"] + k:PC["norm"] + k + 1]) \
                        .then_inc(S_ACT.sem, S_ACT.one(f"hi{k}"))

                def conv_gate(c):
                    for b in range(4):
                        act.wait_ge(CONV_DVE.sem, CONV_DVE.at(l, f"{c}{b}t0"))
                        if b >= 2:
                            act.wait_ge(CONV_DVE.sem, CONV_DVE.at(l, f"{c}{b-2}mul"))
                        nc.scalar.activation(general[:, b % 2], slot(CONV[c])[:, b], ACT.Exp, scale=-1.0) \
                            .then_inc(CONV_ACT.sem, CONV_ACT.one(f"{c}{b}"))

                take_out(l, "dq")
                act.wait_ge(S_PE.sem, S_PE.at(l, "small"))
                sm = mix[0][:, 0:128].rearrange("p (t c) -> p t c", t=TILES)
                nc.scalar.activation(small[:, :, 0:RANK], sm[:, :, 0:RANK], ACT.Copy) \
                    .then_inc(S_ACT.sem, S_ACT.one("lr"))
                nc.scalar.activation(small[:, :, RANK + 1:], sm[:, :, RANK:NSM], ACT.Copy) \
                    .then_inc(S_ACT.sem, S_ACT.one("ba"))
                act.wait_ge(S_ACT.sem, S_ACT.at(l, "ba"))
                nc.scalar.activation(beta[:, :, :], small[:, :, RANK + 1:RANK + 5], ACT.Exp, scale=-1.0) \
                    .then_inc(S_ACT.sem, S_ACT.one("eb"))
                act.wait_ge(S_DVE.sem, S_DVE.at(l, "av"))
                t16 = stat[:, 0:16].rearrange("p (t h) -> p t h", t=TILES)
                nc.scalar.activation(t16, small[:, :, RANK + 5:RANK + 9], ACT.Abs) \
                    .then_inc(S_ACT.sem, S_ACT.one("aab"))
                act.wait_ge(S_ACT.sem, S_ACT.at(l, "aab"))
                nc.scalar.activation(t16, t16, ACT.Exp, scale=-1.0).then_inc(S_ACT.sem, S_ACT.one("ea"))
                act.wait_ge(S_ACT.sem, S_ACT.at(l, "ea"))
                nc.scalar.activation(t16, t16, ACT.Ln, bias=1.0).then_inc(S_ACT.sem, S_ACT.one("la"))
                nc.scalar.activation(sa, pr[:, PR["alog"]:PR["alog"] + 4], ACT.Exp) \
                    .then_inc(S_ACT.sem, S_ACT.one("A"))
                conv_gate("dq")
                take_out(l, "dk")
                act.wait_ge(S_PE.sem, S_PE.at(l, "dec"))
                nc.scalar.activation(decs[:, :, :, :].rearrange("p a t h -> p (a t h)"), mix[3][:, 0:64], ACT.Exp) \
                    .then_inc(S_ACT.sem, S_ACT.one("decs"))
                conv_gate("dk")
                take_out(l, "dv")
                conv_gate("dv")
                take_out(l, "dz")

                def gate(St, step, src, dst, free=None):
                    nc.scalar.activation(dst, src, ACT.Exp, scale=-1.0).then_inc(St.sem, St.one(step))

                for t in T:
                    A, VE, PE_ = D_ACT, D_DVE, D_PE
                    w = lambda st, s, t=t: act.wait_ge(st.sem, st.at(l, f"{t}.{s}"))
                    s = lambda step, t=t: (D_ACT.sem, D_ACT.one(f"{t}.{step}"))
                    w(D_PE, "nat")
                    nc.scalar.activation(U["SQ"][:, 0:4], mh[0], ACT.Square).then_inc(*s("sqq"))
                    nc.scalar.activation(U["SQ"][:, 4:8], mh[1], ACT.Square).then_inc(*s("sqk"))
                    w(D_DVE, "red")
                    nc.scalar.activation(rs[:, 0:8], ss[:, 0:8], ACT.Ln, bias=eps_t[:, :]).then_inc(*s("lnr"))
                    w(D_ACT, "lnr")
                    nc.scalar.activation(rs[:, 0:8], rs[:, 0:8], ACT.Exp, scale=-0.5).then_inc(*s("rr"))
                    nc.scalar.activation(U["VN"], mh[2], ACT.Copy).then_inc(*s("vn"))
                    w(D_PE, "gap")
                    nc.scalar.activation(U["EX"], mh[3], ACT.Exp).then_inc(*s("ex"))
                    w(D_PE, "back")
                    nc.scalar.activation(U["QT"], mh[0], ACT.Copy, scale=HD ** -0.5).then_inc(*s("qT"))
                    nc.scalar.activation(U["QDT"], mh[2], ACT.Copy, scale=HD ** -0.5).then_inc(*s("qdT"))
                    w(D_DVE, "ke")
                    nc.scalar.activation(U["KT"], mh[1], ACT.Copy).then_inc(*s("kT"))
                    for lv in range(2, LEVELS + 1):
                        w(D_PE, f"y{lv}")
                        nc.scalar.activation(U["Y"], mh[3], ACT.Copy).then_inc(*s(f"y{lv}"))
                    w(D_PE, "w")
                    nc.scalar.activation(U["WT"], mh[2], ACT.Copy, scale=-1.0).then_inc(*s("wT"))
                    gz = slot(SLOT["dz"])[:, t].rearrange("p (h c) -> p h c", h=HEADS)
                    if t == 0:
                        act.wait_ge(acc_free, acc_free_after(l, CHUNKS.index("dz"), 3))
                    nc.scalar.activation(U["GATE"], gz, ACT.Exp, scale=-1.0).then_inc(*s("gate"))
                    w(D_PE, "o1")
                    nc.scalar.activation(U["SQO"], mh[2], ACT.Square).then_inc(*s("sqo"))
                    w(D_DVE, "redo")
                    nc.scalar.activation(sa, ss[:, 0:4], ACT.Ln, bias=eps_t[:, :], scale=1.0 / HD) \
                        .then_inc(*s("lno"))
                    w(D_ACT, "lno")
                    nc.scalar.activation(sa, sa, ACT.Exp, scale=-0.5).then_inc(*s("ro"))
                    take_out(l, CHUNKS[4 + t])

                for t in T:
                    w = lambda st, s, t=t: act.wait_ge(st.sem, st.at(l, f"{t}.{s}"))
                    s = lambda step, t=t: (A_ACT.sem, A_ACT.one(f"{t}.{step}"))
                    w(A_PE, "u")
                    nc.scalar.activation(V["T0"], mix[1][:, 0:256], ACT.Abs).then_inc(*s("abs"))
                    w(A_ACT, "abs")
                    nc.scalar.activation(V["T0"], V["T0"], ACT.Exp, scale=-1.0).then_inc(*s("e"))
                    w(A_ACT, "e")
                    nc.scalar.activation(V["T0"], V["T0"], ACT.Ln, bias=1.0).then_inc(*s("l"))
                    w(A_PE, "cum")
                    nc.scalar.activation(V["EB"], mix[0][:, 0:256], ACT.Exp, scale=1.0 / 16).then_inc(*s("eb"))
                    nc.scalar.activation(V["ENB"], mix[0][:, 0:256], ACT.Exp, scale=-1.0 / 16).then_inc(*s("enb"))
                    nc.scalar.activation(V["ER"], mix[0][:, 256:512], ACT.Exp, scale=1.0 / 16).then_inc(*s("er"))
                    w(A_PE, "dec")
                    nc.scalar.activation(V["DECT"], mix[1][:, 0:4], ACT.Exp, scale=1.0 / 16).then_inc(*s("dect"))
                    w(A_PE, "tr")
                    nc.scalar.activation(V["QKT"], mix[2][:, :], ACT.Copy).then_inc(*s("qkT"))
                    gz = slot(SLOT["az"])[:, t].rearrange("p (h c) -> p h c", h=HEADS)
                    nc.scalar.activation(V["GATE"], gz, ACT.Exp, scale=-1.0).then_inc(*s("gate"))
                    w(A_PE, "o")
                    for i in range(2):
                        nc.scalar.activation(V["SQO"][:, i::2], mh[1 + 2 * i][:, i::2], ACT.Square) \
                            .then_inc(*s(f"sqo{i}"))
                    w(A_DVE, "redo")
                    nc.scalar.activation(sa, ss[:, 0:4], ACT.Ln, bias=eps_t[:, :], scale=1.0 / HD) \
                        .then_inc(*s("lno"))
                    w(A_ACT, "lno")
                    nc.scalar.activation(sa, sa, ACT.Exp, scale=-0.5).then_inc(*s("ro"))
                    take_out(l, CHUNKS[8 + t])

                for t in T:
                    w = lambda st, s, t=t: act.wait_ge(st.sem, st.at(l, f"{t}.{s}"))
                    s = lambda step, t=t: (B_ACT.sem, B_ACT.one(f"{t}.{step}"))
                    q, kv = slot(SLOT["bq"])[:, t], slot(SLOT["bkv"])[:, t]
                    if t == 0:
                        act.wait_ge(acc_free, acc_free_after(l, CHUNKS.index("bkv"), 3))
                        act.wait_ge(A_DVE.sem, A_DVE.at(l, f"{TILES-1}.y3"))
                    else:
                        act.wait_ge(B_DVE.sem, B_DVE.at(l, f"{t-1}.y3"))
                    nc.scalar.activation(W["SQ"][:, 0:4].rearrange("p g c -> p (g c)"), q, ACT.Square) \
                        .then_inc(*s("sqq"))
                    nc.scalar.activation(W["SQ"][:, 4:6].rearrange("p g c -> p (g c)"), kv[:, 0:256], ACT.Square) \
                        .then_inc(*s("sqk"))
                    w(B_DVE, "red")
                    nc.scalar.activation(rs[:, 0:6], ss[:, 0:6], ACT.Ln, bias=eps_t[:, :], scale=1.0 / HD) \
                        .then_inc(*s("lnr"))
                    w(B_ACT, "lnr")
                    nc.scalar.activation(rs[:, 0:6], rs[:, 0:6], ACT.Exp, scale=-0.5).then_inc(*s("rr"))
                    w(B_PE, "tr")
                    nc.scalar.activation(W["QT"], mh[0], ACT.Copy, scale=pc[:, PC["gq_b"]:PC["gq_b"] + 1]) \
                        .then_inc(*s("qT"))
                    nc.scalar.activation(kv[:, 0:256], mix[1][:, 0:256], ACT.Copy,
                                         scale=pc[:, PC["gk_b"]:PC["gk_b"] + 1]).then_inc(*s("kT"))
                    n = P * (min(t, 1) + 1)
                    w(B_DVE, "nm")
                    for h in H:
                        nc.scalar.activation(W["SB"][:, h, 0:n], W["SB"][:, h, 0:n], ACT.Exp, bias=sb2[:, h:h + 1],
                                             accum_out=sc[:, h:h + 1]).then_inc(*s(f"p{h}"))
                    w(B_DVE, "es")
                    nc.scalar.activation(sd, sd, ACT.Exp).then_inc(*s("es"))
                    w(B_PE, "pt0")
                    nc.scalar.activation(W["PT"][:, 0:2, 0:n],
                                         mix[0][:, :].rearrange("p (h c) -> p h c", h=2)[:, :, 0:n], ACT.Copy) \
                        .then_inc(*s("PT0"))
                    nc.scalar.activation(W["GATE"], slot(SLOT["bz"])[:, t].rearrange("p (h c) -> p h c", h=HEADS),
                                         ACT.Exp, scale=-1.0).then_inc(*s("gate"))
                    s = lambda step, t=t: (R_ACT.sem, R_ACT.one(f"{t}.{step}"))
                    if t == 0:
                        act.wait_ge(acc_free, acc_free_after(l, CHUNKS.index("ck"), 3))
                    else:
                        act.wait_ge(R_DVE.sem, R_DVE.at(l, f"{t-1}.k"))
                    act.wait_ge(B_DVE.sem, B_DVE.at(l, f"{t}.k"))
                    for i, c in enumerate(("cq", "ck")):
                        nc.scalar.activation(general[:, i], slot(SLOT[c])[:, t], ACT.Square) \
                            .then_inc(*s(("sqq", "sqk")[i]))
                    w(R_DVE, "red")
                    nc.scalar.activation(rs, ss, ACT.Ln, bias=eps_t[:, :], scale=1.0 / DK).then_inc(*s("ln"))
                    w(R_ACT, "ln")
                    nc.scalar.activation(rs, rs, ACT.Exp, scale=-0.5).then_inc(*s("r"))
                    for i, c in enumerate(("q", "k")):
                        w(R_PE, c)
                        g = PC[f"g{c}_c"]
                        nc.scalar.activation(slot(SLOT["c" + c])[:, t], mix[i][:, :], ACT.Copy,
                                             scale=pc[:, g:g + 1]).then_inc(*s(c + "T"))
                    if t % 2:
                        take_out(l, CHUNKS[12 + t // 2])

                def y_hi(k):
                    act.wait_ge(S_PE.sem, S_PE.at(l, f"yT{k}"))
                    nc.scalar.activation(actT_hi[:, k], mix[k % 4][:, :], ACT.Copy,
                                         scale=pc[:, PC["y"] + k:PC["y"] + k + 1]) \
                        .then_inc(S_ACT.sem, S_ACT.one(f"yhi{k}"))

                act.wait_ge(B_DVE.sem, B_DVE.at(l, f"{TILES-1}.y3"))
                act.wait_ge(xcopy, 16)
                act.wait_ge(xout, l * (16 * TILES) + 1)
                act.dma_start(xf, out.rearrange("(t p) n -> p t n", p=P)).then_inc(xres_in, 16)
                act.wait_ge(kt_done, kt_value(l, IN_KTS - 1))
                for k in range(12):
                    y_hi(k)

                for t in back:
                    w = lambda st, s, t=t: act.wait_ge(st.sem, st.at(l, f"{t}.{s}"))
                    s = lambda step, t=t: (C_ACT.sem, C_ACT.one(f"{t}.{step}"))
                    n = t + 1

                    def probs(h):
                        for m in range(2):
                            b = Z["S"][h % 2][m][:, 0:P * n]
                            w(C_DVE, f"m{h}{m}")
                            nc.scalar.activation(b, b, ACT.Exp, bias=stat[:, 32 + 2 * h + m:33 + 2 * h + m],
                                                 accum_out=cden[:, 2 * h + m:2 * h + m + 1]).then_inc(*s(f"p{h}{m}"))

                    for h in H:
                        probs(h)
                        w(C_PE, f"t{h}")
                        nc.scalar.activation(Z["WT"][h % 2][:, 0:n], mh[2][:, 0:n], ACT.Copy).then_inc(*s(f"wT{h}"))
                    nc.scalar.activation(Z["GATE"], slot(SLOT["cz"])[:, t].rearrange("p (h c) -> p h c", h=HEADS),
                                         ACT.Exp, scale=-1.0).then_inc(*s("gate"))
                    w(C_DVE, "os")
                    nc.scalar.activation(Z["SQO"], Z["OS"], ACT.Square).then_inc(*s("sqo"))
                    w(C_DVE, "redo")
                    nc.scalar.activation(stat[:, 44:48], ss[:, 0:4], ACT.Ln, bias=eps_t[:, :], scale=1.0 / HD) \
                        .then_inc(*s("lno"))
                    w(C_ACT, "lno")
                    nc.scalar.activation(stat[:, 44:48], stat[:, 44:48], ACT.Exp, scale=-0.5).then_inc(*s("ro"))
                for k in range(12, 16):
                    y_hi(k)
                for n in T:
                    act.wait_ge(acc_free, acc_free_after(l, 18 + n, 3))
                    act.dma_start(out.rearrange("(t p) n -> p t n", p=P)[:, :, n * GW:n * GW + GW],
                                  xf[:, :, n * GW:n * GW + GW]).then_inc(xout, 16)
            act.wait_ge(xout, 16 * TILES * DEPTH + 1)

        @block.vector
        def _(dve):
            def plain():
                dve.sem_inc(dve_passed, 1)

            dve.memset(eps_t[:, :], EPS)
            dve.memset(small[:, :, RANK:RANK + 1], 1.0)
            dve.wait_ge(lam_in, 16 * DEPTH)
            for l in range(DEPTH):
                for i in range(2):
                    a = slot(4)[:, l, PR["lam"] + 2 * DK * i:PR["lam"] + 2 * DK * i + DK]
                    b = slot(4)[:, l, PR["lam"] + 2 * DK * i + DK:PR["lam"] + 2 * DK * i + 2 * DK]
                    dve.scalar_tensor_tensor(general[:, 0, (2 * l + i) * DK:(2 * l + i + 1) * DK], a, 1.0, b, ALU.mult, ALU.mult,
                                             accum_out=stat[:, 2 * l + i:2 * l + i + 1]).then_inc(lam_steps, 1)
            dve.wait_ge(lam_act, 1)
            e = stat[:, 32:32 + 2 * DEPTH].rearrange("p (l i) -> p l i", i=2)
            dve.tensor_tensor(neg_lam[:, :], e[:, :, 1], e[:, :, 0], ALU.subtract).then_inc(lam_steps, 1)
            dve.wait_ge(lam_steps, 2 * DEPTH + 1)
            dve.tensor_tensor(neg_lam[:, :], neg_lam[:, :], slot(4)[:, 0:DEPTH, PR["linit"]], ALU.subtract) \
                .then_inc(lam_steps, 1)
            dve.wait_ge(consts_in, 16 * (4 + DEPTH))
            dve.tensor_copy(mask_sb[:, :], slot(10).rearrange("p a b -> p (a b)")[:, 0:masks.shape[1]]) \
                .then_inc(lam_steps, 1)
            dve.tensor_scalar(pcol_all[:, :, PC["gq_b"]], pcol_all[:, :, PC["gq_b"]], HD ** -0.5, None, ALU.mult) \
                .then_inc(lam_steps, 1)
            dve.tensor_scalar(pcol_all[:, :, PC["gq_c"]], pcol_all[:, :, PC["gq_c"]], DK ** -0.5, None, ALU.mult) \
                .then_inc(lam_steps, 1)
            yc = pcol_all[:, :, PC["y"] + 12:PC["y"] + 16]
            dve.tensor_tensor(yc, yc, slot(4)[:, 0:DEPTH, PR["one_less"]:PR["one_less"] + 1]
                              .broadcast_to([P, DEPTH, 4]), ALU.mult).then_inc(lam_steps, 1)
            dve.wait_ge(lam_steps, 2 * DEPTH + 6)

            def gate(St, l, t, Zs, tmp):
                dve.wait_ge({id(D_DVE): D_ACT, id(A_DVE): A_ACT, id(B_DVE): B_ACT, id(C_DVE): C_ACT}[id(St)].sem,
                            {id(D_DVE): D_ACT, id(A_DVE): A_ACT, id(B_DVE): B_ACT, id(C_DVE): C_ACT}[id(St)]
                            .at(l, f"{t}.gate"))
                dve.tensor_scalar(tmp, tmp, 1.0, None, ALU.add).then_inc(St.sem, St.one(f"{t}.g1"))
                dve.wait_ge(St.sem, St.at(l, f"{t}.g1"))
                dve.reciprocal(tmp, tmp).then_inc(St.sem, St.one(f"{t}.g2"))
                dve.wait_ge(St.sem, St.at(l, f"{t}.g2"))
                dve.tensor_tensor(Zs, Zs, tmp, ALU.mult).then_inc(St.sem, St.one(f"{t}.g3"))

            with dve.Fori(0, DEPTH) as l:
                def sw(step):
                    dve.wait_ge(S_DVE.sem, S_DVE.at(l, step))

                def si(step):
                    return S_DVE.sem, S_DVE.one(step)

                dve.wait_ge(acc_free, l * (4 * N_ACC) + 4)
                dve.tensor_copy(pc[:, :], pcol_all[:, bass.ds(l, 1)].rearrange("p a n -> p (a n)")).then_inc(*si("pc"))
                dve.tensor_copy(pr[:, :], prow_all[:, bass.ds(l, 1)].rearrange("p a n -> p (a n)")).then_inc(*si("pr"))
                dve.tensor_copy(nlam[:, :], neg_lam[:, bass.ds(l, 1)]).then_inc(*si("lam"))
                dve.tensor_copy(wlr_sb[:, :], wlr_all[:, bass.ds(l, 1)].rearrange("p a n -> p (a n)")) \
                    .then_inc(*si("wlr"))
                dve.wait_ge(xin, 16 * TILES)
                for t in (2, 3):
                    dve.scalar_tensor_tensor(slot(t + 1 if t == 2 else 4).rearrange("p a b -> p (a b)"), xf[:, t], 1.0,
                                             xf[:, t], ALU.mult, ALU.mult, accum_out=ss[:, t:t + 1]) \
                        .then_inc(*si(f"sq{t}"))
                dve.wait_ge(S_ACT.sem, S_ACT.at(l, "r"))
                dve.wait_ge(xout, l * (16 * TILES) + 1)
                for t in T:
                    dve.tensor_scalar(xf[:, t], xf[:, t], rs[:, t:t + 1], None, ALU.mult).then_inc(*si(f"x{t}"))
                for k in range(KT):
                    dve.wait_ge(S_ACT.sem, S_ACT.at(l, f"hi{k}"))
                    dve.scalar_tensor_tensor(actT_lo[:, k], mix[k % 4][:, :],
                                             pc[:, PC["norm"] + k:PC["norm"] + k + 1], actT_hi[:, k].bitcast(F32),
                                             ALU.mult, ALU.subtract).then_inc(*si(f"lo{k}"))

                def conv(c):
                    q = CHUNKS.index(c)
                    for b in range(4):
                        def ci(s):
                            return CONV_DVE.sem, CONV_DVE.one(f"{c}{b}{s}")

                        def cw(s):
                            dve.wait_ge(CONV_DVE.sem, CONV_DVE.at(l, f"{c}{b}{s}"))
                        src, dst = slot(SLOT[c])[:, b], slot(CONV[c])[:, b]
                        tap = [pc[:, PC["conv"] + 4 * (4 * q + b) + i:PC["conv"] + 4 * (4 * q + b) + i + 1]
                               for i in range(4)]
                        dve.wait_ge(acc_free, acc_free_after(l, q, b))
                        dve.tensor_scalar(dst, src, tap[3], None, ALU.mult).then_inc(*ci("t3"))
                        for i, prev in ((2, "t3"), (1, "t2"), (0, "t1")):
                            cw(prev)
                            d = 3 - i
                            dve.scalar_tensor_tensor(dst[:, d:], src[:, 0:SEQ - d], tap[i], dst[:, d:],
                                                     ALU.mult, ALU.add).then_inc(*ci(f"t{i}"))
                        dve.wait_ge(CONV_ACT.sem, CONV_ACT.at(l, f"{c}{b}"))
                        dve.tensor_scalar(general[:, b % 2], general[:, b % 2], 1.0, None, ALU.add) \
                            .then_inc(*ci("one"))
                        cw("one")
                        dve.reciprocal(general[:, b % 2], general[:, b % 2]).then_inc(*ci("rec"))
                        cw("rec")
                        dve.tensor_tensor(dst, dst, general[:, b % 2], ALU.mult).then_inc(*ci("mul"))

                dve.wait_ge(S_ACT.sem, S_ACT.at(l, "eb"))
                dve.tensor_scalar(beta[:, :, :], beta[:, :, :], 1.0, None, ALU.add).then_inc(*si("b1"))
                sw("b1")
                dve.reciprocal(beta[:, :, :], beta[:, :, :]).then_inc(*si("beta"))
                sw("beta")
                dve.tensor_scalar(nbeta[:, :, :], beta[:, :, :], -1.0, None, ALU.mult).then_inc(*si("nbeta"))
                av = small[:, :, RANK + 5:RANK + 9]
                dve.tensor_tensor(av, av, pr[:, PR["dtb"]:PR["dtb"] + 4].unsqueeze(1)
                                  .broadcast_to([P, TILES, HEADS]), ALU.add).then_inc(*si("av"))
                dve.wait_ge(S_ACT.sem, S_ACT.at(l, "A"))
                t16 = stat[:, 0:16].rearrange("p (t h) -> p t h", t=TILES)
                dve.scalar_tensor_tensor(glog[:, :, :], av, 0.0, t16, ALU.max, ALU.add).then_inc(*si("sp"))
                sw("sp")
                dve.tensor_scalar(glog[:, :, :], glog[:, :, :], -1.0, None, ALU.mult).then_inc(*si("glog"))
                sw("glog")
                dve.tensor_tensor(glog[:, :, :], glog[:, :, :], sa.unsqueeze(1).broadcast_to([P, TILES, HEADS]),
                                  ALU.mult).then_inc(*si("gA"))
                conv("dq")
                conv("dk")
                conv("dv")
                dve.memset(U["S"][0], 0.0).then_inc(*si("zero_gdn"))

                for t in T:
                    w = lambda st, s, t=t: dve.wait_ge(st.sem, st.at(l, f"{t}.{s}"))
                    s = lambda step, t=t: (D_DVE.sem, D_DVE.one(f"{t}.{step}"))
                    b4, nb4 = beta[:, t], nbeta[:, t]
                    if t:
                        w2 = D_DVE.at(l, f"{t-1}.y3y")
                        dve.wait_ge(D_DVE.sem, w2)
                    dve.tensor_tensor(U["AG"], heads(after), cols(glog[:, t]), ALU.mult).then_inc(*s("ag"))
                    w(D_ACT, "sqk")
                    dve.reduce_sum(ss[:, 0:8], U["SQ"], AX.X).then_inc(*s("red"))
                    w(D_ACT, "rr")
                    dve.tensor_tensor(U["QN"], mh[0], cols(rs[:, 0:4]), ALU.mult).then_inc(*s("qn"))
                    dve.tensor_tensor(U["KN"], mh[1], cols(rs[:, 4:8]), ALU.mult).then_inc(*s("kn"))
                    w(D_DVE, "qn")
                    dve.tensor_tensor(U["QD"], U["QN"], cols(decs[:, 0, t]), ALU.mult).then_inc(*s("qd"))
                    w(D_DVE, "kn")
                    dve.tensor_tensor(U["KB"], U["KN"], cols(decs[:, 0, t]), ALU.mult).then_inc(*s("kb"))
                    dve.tensor_tensor(U["KE"], U["KN"], cols(decs[:, 1, t]), ALU.mult).then_inc(*s("ke"))
                    w(D_ACT, "ex")
                    dve.tensor_tensor(U["EI"], U["EX"], heads(upto), ALU.mult).then_inc(*s("ei"))
                    w(D_DVE, "ei")
                    for h in H:
                        dve.scalar_tensor_tensor(U["EX"][:, h], U["EX"][:, h], nb4[:, h:h + 1], before,
                                                 ALU.mult, ALU.mult).then_inc(*s(f"es{h}"))
                    w(D_DVE, "es3")
                    w(D_PE, "kk")
                    dve.tensor_tensor(U["MT"], mh[0], U["EX"], ALU.mult).then_inc(*s("mt"))
                    w(D_PE, "kq")
                    dve.tensor_tensor(U["QK"], mh[1], U["EI"], ALU.mult).then_inc(*s("qk"))
                    dve.tensor_copy(U["X"], heads(ident)).then_inc(*s("xi"))
                    dve.tensor_copy(U["XT"], heads(ident)).then_inc(*s("xti"))
                    w(D_DVE, "xti")
                    plain()
                    dve.copy_predicated(U["XT"], heads(m_xt[0]), U["MT"]).then_inc(*s("xt1"))
                    w(D_PE, "m1")
                    plain()
                    dve.copy_predicated(U["X"], heads(m_x[0]), mh[2]).then_inc(*s("x1"))
                    for lv in range(2, LEVELS + 1):
                        if lv < LEVELS:
                            w(D_PE, f"p{lv}")
                            w(D_DVE, f"x{lv-1}")
                            plain()
                            dve.copy_predicated(U["X"], heads(m_x[lv - 1]), mh[0]).then_inc(*s(f"x{lv}"))
                        w(D_PE, f"pt{lv}")
                        w(D_DVE, f"xt{lv-1}")
                        plain()
                        dve.copy_predicated(U["XT"], heads(m_xt[lv - 1]), mh[1]).then_inc(*s(f"xt{lv}"))
                    gz = slot(SLOT["dz"])[:, t].rearrange("p (h c) -> p h c", h=HEADS)
                    gate(D_DVE, l, t, gz, U["GATE"])
                    for j in range(2):
                        r = slice(CH * j, CH * j + CH)
                        w(D_PE, f"v{j}")
                        dve.tensor_tensor(U["VW"][r], mh[3][r], cols(b4[r], parts=CH), ALU.mult) \
                            .then_inc(*s(f"v{j}"))
                        w(D_PE, f"s{j}")
                        for h in H:
                            dve.scalar_tensor_tensor(U["S"][1 - j][:, h], U["S"][j][:, h],
                                                     decs[:, 2 + j, t, h:h + 1], mh[j][:, h],
                                                     ALU.mult, ALU.add).then_inc(*s(f"s{j}{h}"))
                    w(D_ACT, "sqo")
                    dve.reduce_sum(ss[:, 0:4], U["SQO"], AX.X).then_inc(*s("redo"))
                    w(D_ACT, "ro")
                    w(D_DVE, "g3")
                    for h in H:
                        dve.scalar_tensor_tensor(gz[:, h], mh[2][:, h], sa[:, h:h + 1], gz[:, h],
                                                 ALU.mult, ALU.mult).then_inc(*s(("y0", "y1", "y2y", "y3y")[h]))

                dve.wait_ge(D_DVE.sem, D_DVE.at(l, f"{TILES-1}.y3y"))
                dve.memset(V["S"][:, 0], 0.0).then_inc(A_DVE.sem, A_DVE.one("zero_s"))
                dve.memset(V["AT"], 0.0).then_inc(A_DVE.sem, A_DVE.one("zero_a"))
                for t in T:
                    w = lambda st, s, t=t: dve.wait_ge(st.sem, st.at(l, f"{t}.{s}"))
                    s = lambda step, t=t: (A_DVE.sem, A_DVE.one(f"{t}.{step}"))
                    q, k = slot(SLOT["aq"])[:, t, 0:256], slot(SLOT["aq"])[:, t, 256:512]
                    w(A_PE, "lrT")
                    dve.tensor_copy(V["LR"], mix[0][0:RANK + 1, 0:P]).then_inc(*s("lr"))
                    w(A_ACT, "l")
                    dve.scalar_tensor_tensor(V["G"], mix[1][:, 0:256], 0.0, V["T0"], ALU.min, ALU.subtract) \
                        .then_inc(*s("g"))
                    w(A_ACT, "er")
                    if t == 0:
                        dve.wait_ge(acc_free, acc_free_after(l, CHUNKS.index("av"), 3))
                    dve.scalar_tensor_tensor(V["QD"], V["EB"], DK ** -0.5, q, ALU.mult, ALU.mult).then_inc(*s("qd"))
                    dve.tensor_tensor(V["KI"], V["ENB"], k, ALU.mult).then_inc(*s("ki"))
                    dve.tensor_tensor(V["KE"], V["ER"], k, ALU.mult).then_inc(*s("ke"))
                    w(A_PE, "a")
                    w(A_DVE, "ke")
                    for i in range(2):
                        plain()
                        dve.copy_predicated(V["AT"][:, i::2], heads(m_upto)[:, 0:2], mh[3 - i][:, i::2]) \
                            .then_inc(*s(f"at{i}"))
                    w(A_PE, "us")
                    w(A_ACT, "dect")
                    w(A_DVE, "at1")
                    for j in range(2):
                        if j:
                            w(A_DVE, "s01")
                        for p in range(2):
                            dve.scalar_tensor_tensor(V["S"][:, (2 * t + j + 1) % 3, p], V["S"][:, (2 * t + j) % 3, p],
                                                     V["DECT"][:, 2 * p + j:2 * p + j + 1], mh[j][:, p],
                                                     ALU.mult, ALU.add).then_inc(*s(f"s{j}{p}"))
                    gz = slot(SLOT["az"])[:, t].rearrange("p (h c) -> p h c", h=HEADS)
                    gate(A_DVE, l, t, gz, V["GATE"])
                    w(A_ACT, "sqo1")
                    dve.reduce_sum(ss[:, 0:4], V["SQO"], AX.X).then_inc(*s("redo"))
                    w(A_ACT, "ro")
                    w(A_DVE, "g3")
                    for h in H:
                        dve.scalar_tensor_tensor(gz[:, h], mh[3 if h % 2 else 1][:, h], sa[:, h:h + 1], gz[:, h],
                                                 ALU.mult, ALU.mult).then_inc(*s(f"y{h}"))

                for t in T:
                    w = lambda st, s, t=t: dve.wait_ge(st.sem, st.at(l, f"{t}.{s}"))
                    s = lambda step, t=t: (B_DVE.sem, B_DVE.one(f"{t}.{step}"))
                    q = slot(SLOT["bq"])[:, t].rearrange("p (h c) -> p h c", h=HEADS)
                    k = slot(SLOT["bkv"])[:, t, 0:256].rearrange("p (h c) -> p h c", h=2)
                    n = P * (min(t, 1) + 1)
                    w(B_ACT, "sqk")
                    dve.reduce_sum(ss[:, 0:6], W["SQ"], AX.X).then_inc(*s("red"))
                    w(B_ACT, "rr")
                    dve.tensor_tensor(q, q, cols(rs[:, 0:4]), ALU.mult).then_inc(*s("q"))
                    dve.tensor_tensor(k, k, cols(rs[:, 4:6]), ALU.mult).then_inc(*s("k"))
                    for h in H:
                        w(B_PE, f"s{h//2}")
                        dve.scalar_tensor_tensor(W["SB"][:, h, 0:n], win[:, 256 - n:256], -SLOPES_B[h],
                                                 mix[2 + h // 2][:, 256 * (h % 2):256 * (h % 2) + n],
                                                 ALU.mult, ALU.add).then_inc(*s(f"b{h}"))
                    w(B_DVE, "b3")
                    dve.reduce_max(sa, W["SB"][:, :, 0:n], AX.X).then_inc(*s("mx"))
                    w(B_DVE, "mx")
                    dve.tensor_tensor(sa, sa, pr[:, PR["sink"]:PR["sink"] + 4], ALU.max).then_inc(*s("mxs"))
                    w(B_DVE, "mxs")
                    dve.tensor_scalar(sb2, sa, -1.0, None, ALU.mult).then_inc(*s("nm"))
                    w(B_DVE, "nm")
                    dve.tensor_tensor(sd, sb2, pr[:, PR["sink"]:PR["sink"] + 4], ALU.add).then_inc(*s("es"))
                    w(B_ACT, "es")
                    dve.tensor_tensor(se, sc, sd, ALU.add).then_inc(*s("den"))
                    w(B_DVE, "den")
                    dve.reciprocal(se, se).then_inc(*s("rd"))
                    w(B_PE, "pt1")
                    dve.tensor_copy(W["PT"][:, 2:4, 0:n],
                                    mix[1][:, :].rearrange("p (h c) -> p h c", h=2)[:, :, 0:n]).then_inc(*s("PT1"))
                    gz = slot(SLOT["bz"])[:, t].rearrange("p (h c) -> p h c", h=HEADS)
                    gate(B_DVE, l, t, gz, W["GATE"])
                    w(B_PE, "pv")
                    w(B_DVE, "g3")
                    for h in H:
                        dve.scalar_tensor_tensor(gz[:, h], mh[2][:, h], se[:, h:h + 1], gz[:, h],
                                                 ALU.mult, ALU.mult).then_inc(*s(f"y{h}"))
                    s = lambda step, t=t: (R_DVE.sem, R_DVE.one(f"{t}.{step}"))
                    w(R_ACT, "sqk")
                    dve.reduce_sum(ss, RQ, AX.X).then_inc(*s("red"))
                    w(R_ACT, "r")
                    for i, c in enumerate("qk"):
                        v = slot(SLOT["c" + c])[:, t].rearrange("p (g c) -> p g c", c=DK)
                        dve.tensor_tensor(v, v, cols(rs[:, 8 * i:8 * i + 8], n=DK), ALU.mult).then_inc(*s(c))

                def y_lo(k):
                    dve.wait_ge(S_ACT.sem, S_ACT.at(l, f"yhi{k}"))
                    dve.scalar_tensor_tensor(actT_lo[:, k], mix[k % 4][:, :], pc[:, PC["y"] + k:PC["y"] + k + 1],
                                             actT_hi[:, k].bitcast(F32), ALU.mult, ALU.subtract) \
                        .then_inc(*si(f"ylo{k}"))

                def add(q, n, last_kt):
                    for b in range(4):
                        wait_acc(dve, l, q, b, last_kt)
                        xs = xf[:, b, n * GW:n * GW + GW]
                        dve.tensor_tensor(xs, acc[b][:, :], xs, ALU.add).then_inc(acc_free, 1)

                for k in range(12):
                    y_lo(k)
                for t in back:
                    w = lambda st, s, t=t: dve.wait_ge(st.sem, st.at(l, f"{t}.{s}"))
                    s = lambda step, t=t: (C_DVE.sem, C_DVE.one(f"{t}.{step}"))
                    n = P * (t + 1)
                    for h in H:
                        S = Z["S"][h % 2]
                        w(C_PE, f"s{h}")
                        if h >= 2:
                            w(C_PE, f"t{h-2}")
                        for m in range(2):
                            dve.scalar_tensor_tensor(S[m][:, 0:n], dist[:, 384 - P * t:384 - P * t + n], -SLOPES_C[h],
                                                     mix[m][:, 0:n], ALU.mult, ALU.add).then_inc(*s(f"b{h}{m}"))
                        for m in range(2):
                            w(C_DVE, f"b{h}{m}")
                            dve.tensor_reduce(stat[:, 32 + 2 * h + m:33 + 2 * h + m], S[m][:, 0:n], AX.X, ALU.max,
                                              negate=True).then_inc(*s(f"m{h}{m}"))
                        w(C_ACT, f"p{h}1")
                        dve.reciprocal(stat[:, 16 + 2 * h:18 + 2 * h], cden[:, 2 * h:2 * h + 2]) \
                            .then_inc(*s(f"r{h}"))
                        w(C_DVE, f"r{h}")
                        dve.scalar_tensor_tensor(stat[:, 24 + h:25 + h], stat[:, 17 + 2 * h:18 + 2 * h],
                                                 cden[:, 2 * h:2 * h + 1], nlam[:, :], ALU.mult, ALU.mult) \
                            .then_inc(*s(f"c{h}"))
                        w(C_DVE, f"c{h}")
                        dve.scalar_tensor_tensor(S[0][:, 0:n], S[1][:, 0:n], stat[:, 24 + h:25 + h], S[0][:, 0:n],
                                                 ALU.mult, ALU.add).then_inc(*s(f"w{h}"))
                    gz = slot(SLOT["cz"])[:, t].rearrange("p (h c) -> p h c", h=HEADS)
                    gate(C_DVE, l, t, gz, Z["GATE"])
                    w(C_PE, "v3")
                    dve.tensor_tensor(Z["OS"], mh[3], cols(stat[:, 16:24:2]), ALU.mult).then_inc(*s("os"))
                    w(C_ACT, "sqo")
                    dve.reduce_sum(ss[:, 0:4], Z["SQO"], AX.X).then_inc(*s("redo"))
                    w(C_ACT, "ro")
                    w(C_DVE, "g3")
                    for h in H:
                        dve.scalar_tensor_tensor(gz[:, h], Z["OS"][:, h], stat[:, 44 + h:45 + h], gz[:, h],
                                                 ALU.mult, ALU.mult).then_inc(*s(f"y{h}"))
                    if t == TILES - 1:
                        dve.wait_ge(xres_in, l * 16 + 16)
                    add(14 + TILES - 1 - t, TILES - 1 - t, IN_KTS + 12 * (TILES - t) - 1)
                for k in range(12, 16):
                    y_lo(k)
                for n in T:
                    add(18 + n, n, IN_KTS + OUT_KTS + 4 * n + 3)


def constants():
    s, c = np.arange(P)[:, None], np.arange(P)[None, :]
    same = (s // CH) == (c // CH)
    f = [s == c, same & (s <= c), same & (s > c), same & (s < c), (s < CH) & (c >= 0), (s >= CH) & (c >= 0)]
    f = [a.astype(np.float32) for a in f]
    d = s + P - np.arange(2 * P)[None, :]
    f.append(np.where((d >= 0) & (d < P), d, BIG).astype(np.float32))
    d = s + 3 * P - np.arange(7 * P)[None, :]
    f.append(np.where(d >= 0, d, BIG).astype(np.float32))
    u = []
    for lv in range(LEVELS):
        b = 2 ** lv
        low = ((s // (2 * b)) == (c // (2 * b))) & ((s // b) % 2 == 1) & ((c // b) % 2 == 0)
        u.append(low)
    u = [a.astype(np.float32) for a in u]
    u += [np.ascontiguousarray(a.T) for a in u]
    u.append((same & (s <= c)).astype(np.float32))
    return np.concatenate(f, 1), np.concatenate(u, 1)


def kernel(**inputs):
    import concourse.bacc as bacc
    from concourse.bass_utils import run_bass_kernel_spmd

    a = {k: np.asarray(v) for k, v in inputs.items()}
    L = DEPTH
    win = a["w_in"].reshape(L, KT, P, -1)
    parts = [win[..., OFF[c]:OFF[c] + GW] for c in CHUNKS]
    wo = a["w_out"].reshape(L, 4, HEADS, P, D_MODEL)[:, OUT_GROUPS].reshape(L, KT, P, D_MODEL)
    parts += [wo[:, 0:12, :, n * GW:n * GW + GW] for n in range(TILES)]
    parts += [wo[:, 12:16, :, n * GW:n * GW + GW] for n in range(TILES)]
    ws = np.concatenate(parts, 1).reshape(L, PAIRS, 2, P, GW).transpose(0, 1, 3, 2, 4)
    wstream = np.ascontiguousarray(ws).reshape(L * PAIRS, P, 2 * GW)
    sm = np.concatenate([win[..., OFF["alr"]:OFF["alr"] + RANK], win[..., OFF["dbeta"]:OFF["dbeta"] + 2 * HEADS]], -1)
    wsmall = np.ascontiguousarray(sm.transpose(0, 2, 1, 3)).reshape(L, P, KT * NSM)
    pcol = np.zeros((L, P, NPC), np.float32)
    pcol[:, :, 0:KT] = a["norm_g"].reshape(L, KT, P).transpose(0, 2, 1)
    pcol[:, :, 16:20] = a["gdn_norm_g"][:, :, None]
    pcol[:, :, 20:24] = 1.0
    pcol[:, :, 24:28] = a["gla_norm_g"][:, :, None]
    pcol[:, :, 28:32] = a["diff_subln_g"][:, :, None]
    pcol[:, :, PC["gq_b"]] = a["swa_q_norm_g"]
    pcol[:, :, PC["gk_b"]] = a["swa_k_norm_g"]
    for i in range(2):
        pcol[:, DK * i:DK * i + DK, PC["gq_c"]] = a["diff_q_norm_g"]
        pcol[:, DK * i:DK * i + DK, PC["gk_c"]] = a["diff_k_norm_g"]
    pcol[:, :, PC["conv"]:] = a["gdn_conv_w"].reshape(L, 4, 12, P).transpose(0, 3, 2, 1).reshape(L, P, 48)
    prow = np.zeros((L, NPR), np.float32)
    prow[:, 0:4] = a["swa_sinks"]
    prow[:, 4:8] = a["gdn_A_log"]
    prow[:, 8:12] = a["gdn_dt_bias"]
    prow[:, 12:12 + 4 * DK] = a["diff_lambda"].reshape(L, 4 * DK)
    init = [0.8 - 0.6 * math.exp(-0.3 * l) for l in range(L)]
    prow[:, PR["linit"]] = init
    prow[:, PR["one_less"]] = [1.0 - i for i in init]
    wlr = np.concatenate([a["gla_w_lr2"], a["gla_b_lr2"][:, None, :]], 1)
    cf, masks = constants()
    arrays = dict(x=a["x"].reshape(SEQ, D_MODEL), wstream=wstream, wsmall=wsmall, pcol=pcol, prow=prow,
                  wlr=wlr, cf=cf, masks=masks)
    arrays = {f"in_{k}": np.ascontiguousarray(v) for k, v in arrays.items()}

    nc = bacc.Bacc("TRN2", target_bir_lowering=False, num_devices=1)
    args = [nc.dram_tensor(k, v.shape, mybir.dt.from_np(v.dtype), kind="ExternalInput").ap()
            for k, v in arrays.items()]
    args.append(nc.dram_tensor("out_x", (SEQ, D_MODEL), F32, kind="ExternalOutput").ap())
    hybrid_trunk(nc, *args)
    r = run_bass_kernel_spmd(nc, [arrays], core_ids=[0])
    return r.results[0]["out_x"].reshape(1, SEQ, D_MODEL)
```

```python
import math
from contextlib import ExitStack

import concourse.bass as bass
import numpy as np
from concourse import mybir

F32 = mybir.dt.float32
F32R = mybir.dt.float32r
U8 = mybir.dt.uint8
ALU = mybir.AluOpType
ACT = mybir.ActivationFunctionType
AX = mybir.AxisListType

P = 128
DEPTH, SEQ, D_MODEL = 2, 512, 2048
TILES = SEQ // P
KT = D_MODEL // P
GW = 512
HEADS, HD, DK = 4, 128, 64
CH = 64
RANK = 16
EPS = 1e-6
BIG = 3.0e38
SLOPES_B = [2.0 ** -(n + 1) for n in range(0, 2 * HEADS, 2)]
SLOPES_C = [2.0 ** -(n + 1) for n in range(1, 2 * HEADS, 2)]

OFF = dict(aq=0, av=512, alr=1024, az=1040, bq=1552, bkv=2064, bz=2576, cq=3088, ck=3600, cv=4112, cz=4624,
           dq=5136, dk=5648, dv=6160, dbeta=6672, da=6676, dz=6680)
CHUNKS = ["dq", "dk", "dv", "dz", "bz", "az", "aq", "av", "bq", "bkv", "cq", "ck", "cv", "cz"]
OUT_GROUPS = [3, 0, 1, 2]
IN_KTS = len(CHUNKS) * KT
OUT_KTS = TILES * 3 * HEADS
LAST_KTS = TILES * HEADS
LAYER_KTS = IN_KTS + OUT_KTS + LAST_KTS
PAIRS = LAYER_KTS // 2
RAW, RING = 4, 4
NSM = RANK + 2 * HEADS

SLOT = dict(dq=4, dk=5, dv=8, dz=3, bz=4, az=5, aq=6, av=7, bq=8, bkv=9, cq=10, ck=11, cv=12, cz=13)
FIRST_SLOT, SLOTS = 3, 11
CONV = dict(dq=10, dk=11, dv=12)
XSLOT = 6

PC = dict(norm=0, y=16, gq_b=32, gk_b=33, gq_c=34, gk_c=35, conv=36)
NPC = 36 + 12 * 4
PR = dict(sink=0, alog=4, dtb=8, lam=12, linit=12 + 4 * DK, one_less=13 + 4 * DK)
NPR = 14 + 4 * DK
LEVELS = 6


class Steps:

    def __init__(self, sem, steps, before=0):
        self.sem, self.steps, self.before = sem, steps, before
        self.place = {s: i + 1 for i, s in enumerate(steps)}
        assert len(self.place) == len(steps)
        self.given = 0

    def at(self, layer, step):
        return layer * len(self.steps) + (self.before + self.place[step])

    def before_layer(self, layer):
        return layer * len(self.steps) + self.before

    def one(self, step):
        assert self.steps[self.given % len(self.steps)] == step, (self.steps[self.given % len(self.steps)], step)
        self.given += 1
        return 1


def names(fmt, *ranges):
    out = [""]
    for r in ranges:
        out = [f"{a}{'.' if a else ''}{x}" for a in out for x in r]
    return [fmt + x for x in out] if fmt else out


T = range(TILES)
H = range(HEADS)

GDN_PE = ("gap nat back kk kq m1 y2 tx2 p2 y3 tx3 p3 y4 tx4 p4 y5 tx5 p5 y6 tx6 pt6 w u v0 s0 v1 s1 o").split()
GDN_ACT = "sqq sqk lnr rr vn ex qT qdT kT y2 y3 y4 y5 y6 wT gate sqo lno ro".split()
GDN_DVE = ("ag red qn kn qd kb ke ei es0 es1 es2 es3 mt qk xi x1 xt2 x2 xt3 x3 xt4 x4 xt5 x5 xt6 xt7 "
           "g1 g2 g3 ub v00 v01 v02 v03 s00 s01 s02 s03 v10 v11 v12 v13 s10 s11 s12 s13 redo y0 y1 y2 y3").split()
GLA_PE = "u cum dec tr a us o".split()
GLA_ACT = "abs e l eb enb er dect qkT gate sqo0 sqo1 lno ro".split()
GLA_DVE = "g qd ki ke at0 at1 s00 s01 s10 s11 g1 g2 g3 redo y0 y1 y2 y3".split()
SWA_PE = "tr s0 s1 pt0 pt1 pv".split()
SWA_ACT = "gate qT kT p0 p1 p2 p3 es PT0".split()
SWA_DVE = "b0 b1 b2 b3 mx mxs nm es g1 g2 g3 den rd PT1 y0 y1 y2 y3".split()
PREP_PE = "q k".split()
PREP_ACT = "qT kT".split()
NORM_ACT = "bq bk cq ck lnb rb lnc rc".split()
NORM_DVE = "redb redc bq bk cq ck".split()
DIF_PE = ["s0", "s1", "t0", "v0", "s2", "t1", "v1", "s3", "t2", "v2", "t3", "v3"]
DIF_ACT = ["gate"] + [x for h in H for x in (f"p{h}0", f"p{h}1", f"wT{h}")] + ["sqo", "lno", "ro"]
DIF_DVE = [x for h in H for x in (f"b{h}0", f"b{h}1", f"m{h}0", f"m{h}1", f"r{h}", f"c{h}", f"w{h}")] + \
    "g1 g2 g3 os redo y0 y1 y2 y3".split()


def hybrid_trunk(nc, x, wstream, wsmall, pcol, prow, wlr, cf, masks, out):
    ctx = ExitStack()
    with ctx:
        def sb(name, shape, dt=F32):
            return ctx.enter_context(nc.sbuf_tensor(name, shape, dt))

        def sem(name):
            return ctx.enter_context(nc.semaphore(name))

        slots = sb("slots", [P, SLOTS, TILES, GW])
        actT_hi = sb("actT_hi", [P, KT, SEQ], F32R)
        actT_lo = sb("actT_lo", [P, KT, SEQ], F32R)
        w_raw = sb("w_raw", [P, RAW, 2, GW])
        w_hi = sb("w_hi", [P, RING, GW], F32R)
        w_lo = sb("w_lo", [P, RING, GW], F32R)
        ws_raw = sb("ws_raw", [P, KT * NSM])
        ws_hi = sb("ws_hi", [P, KT * NSM + P - NSM], F32R)
        ws_lo = sb("ws_lo", [P, KT * NSM + P - NSM], F32R)
        zeros = sb("zeros", [P, 1])
        general = sb("general", [P, 2, GW])
        cf_sb = sb("cf_sb", [P, cf.shape[1]])
        mask_sb = sb("mask_sb", [P, masks.shape[1] + P], U8)
        pcol_all = sb("pcol_all", [P, DEPTH, NPC])
        prow_all = sb("prow_all", [P, DEPTH, 12])
        pc = sb("pc", [P, NPC])
        pr = sb("pr", [P, 12])
        neg_lam = sb("neg_lam", [P, DEPTH])
        nlam = sb("nlam", [P, 1])
        wlr_sb = sb("wlr_sb", [NSM + 1, HEADS * DK])
        smT = sb("smT", [NSM + 1, SEQ])
        small = sb("small", [P, TILES, 2 * HEADS])
        stat = sb("stat", [P, 96])
        beta = sb("beta", [P, TILES, HEADS])
        nbeta = sb("nbeta", [P, TILES, HEADS])
        glog = sb("glog", [P, TILES, HEADS])
        decs = sb("decs", [P, 4, TILES, HEADS])
        eps_t = sb("eps_t", [P, 1])

        def slot(n):
            return slots[:, n - FIRST_SLOT]

        xf = slots[:, XSLOT - FIRST_SLOT:XSLOT - FIRST_SLOT + 4].rearrange("p a b c -> p (a b c)") \
            .rearrange("p (t n) -> p t n", t=TILES)

        def unit(n, k):
            return slot(n)[:, k].rearrange("p (h c) -> p h c", h=HEADS)

        gen = [general[:, i].rearrange("p (h c) -> p h c", h=HEADS) for i in range(2)]

        ident = cf_sb[:, 0:128]
        upto = cf_sb[:, 128:256]
        after = cf_sb[:, 256:384]
        before = cf_sb[:, 384:512]
        half = [cf_sb[:, 512:640], cf_sb[:, 640:768]]
        win = cf_sb[:, 768:1024]
        dist = cf_sb[:, 1024:1024 + 896]
        m_x = [mask_sb[:, 128 * i:128 * i + 128] for i in range(LEVELS - 1)]
        m_xt6 = mask_sb[:, 128 * (LEVELS - 1):128 * LEVELS]
        m_upto = mask_sb[:, 128 * LEVELS:128 * LEVELS + 128]

        def heads(ap):
            return ap.unsqueeze(1).broadcast_to([P, HEADS, 128])

        def cols(ap, n=128, parts=P):
            return ap.unsqueeze(2).broadcast_to([parts, ap.shape[1], n])

        acc = [ctx.enter_context(nc.psum_tensor(f"acc{i}", [P, GW], F32)) for i in range(4)]
        mix = [ctx.enter_context(nc.psum_tensor(f"mix{i}", [P, GW], F32)) for i in range(4)]
        mh = [m[:, :].rearrange("p (h c) -> p h c", h=HEADS) for m in mix]

        U = dict(S=(unit(8, 0), unit(8, 1)), KB=unit(8, 2), KE=unit(8, 3), VN=unit(9, 0), QDT=unit(9, 1),
                 QK=unit(9, 2), AG=unit(9, 2), UB=unit(13, 2), MT=unit(9, 3), QD=unit(9, 3), GATE=unit(9, 3),
                 X=unit(13, 0), XT=unit(13, 1), QN=unit(13, 2), QT=unit(13, 2), Y=unit(13, 2),
                 KN=unit(13, 3), KT=unit(13, 3), WT=unit(13, 3), EX=gen[0], VW=gen[0], EI=gen[1], SQO=gen[1])
        U["SQ"] = slot(13)[:, 0:2].rearrange("p a (h c) -> p (a h) c", h=HEADS)
        s12 = slot(12).rearrange("p a b -> p (a b)")
        s13 = slot(13).rearrange("p a b -> p (a b)")
        V = dict(T0=s12[:, 128:384], G=s12[:, 384:640], EB=s12[:, 640:896],
                 ENB=s12[:, 896:1152], ER=s12[:, 1152:1408], DECT=s12[:, 1408:1412],
                 QD=s13[:, 0:256], KI=s13[:, 256:512], KE=s13[:, 512:768],
                 QKT=s12[:, 1536:2048], GATE=unit(13, 3), SQO=gen[1], AT=gen[0],
                 S=s13[:, 768:1536].rearrange("p (s p2 c) -> p s p2 c", s=3, p2=2))
        s6 = slot(6).rearrange("p a b -> p (a b)")
        s7 = slot(7).rearrange("p a b -> p (a b)")
        W = dict(SQ=s6[:, 0:768].rearrange("p (g c) -> p g c", c=HD), QT=unit(6, 2), GATE=unit(6, 3),
                 SB=s7[:, 0:1024].rearrange("p (h c) -> p h c", h=HEADS),
                 PT=s7[:, 1024:2048].rearrange("p (h c) -> p h c", h=HEADS))
        RQ = general[:, :, :].rearrange("p a (g c) -> p (a g) c", c=DK)
        f3 = [slot(3)[:, i] for i in range(4)]
        Z = dict(S=((f3[0], f3[1]), (f3[2], f3[3])), WT=(unit(4, 0), unit(4, 1)), OS=unit(4, 2), SQO=unit(4, 3),
                 GATE=unit(5, 0))
        ss, rs = stat[:, 0:16], stat[:, 16:32]
        sa, sb2, sc, sd, se = (stat[:, 32 + 4 * i:36 + 4 * i] for i in range(5))
        cden = stat[:, 52:60]
        ssb, rsb = stat[:, 64:70], stat[:, 72:78]

        consts_in, params_in, xcopy = sem("consts_in"), sem("params_in"), sem("xcopy")
        xin = [sem(f"xin{t}") for t in T]
        raw_in = [sem(f"raw_in{i}") for i in range(RAW)]
        zeros_done, ones_done, masks_done = sem("zeros_done"), sem("ones_done"), sem("masks_done")
        wlr_in, masks_in = sem("wlr_in"), sem("masks_in")
        dve_passed, pe_passed = sem("dve_passed"), sem("pe_passed")
        raw_used, hi_done, w_ready = sem("raw_used"), sem("hi_done"), sem("w_ready")
        ws_hi_done, ws_ready = sem("ws_hi_done"), sem("ws_ready")
        ws_in = sem("ws_in")
        kt_done = sem("kt_done")
        acc_ready, acc_free = sem("acc_ready"), sem("acc_free")
        xres_in, xout = sem("xres_in"), sem("xout")
        lam_steps = sem("lam_steps")
        lam_act = sem("lam_act")

        N_ACC = len(CHUNKS) + 2 * TILES

        def kt_value(l, kt):
            return l * LAYER_KTS + (RING + kt + 1)

        def acc_free_value(l, q, b):
            return l * (4 * N_ACC) + (4 * q + b + 1)

        def acc_free_after(l, q, b):
            return l * (4 * N_ACC) + (4 * q + b + 5)

        def wait_acc(eng, l, q, b, last_kt):
            if b < 3:
                eng.wait_ge(acc_ready, l * (3 * N_ACC) + (3 * q + b + 1))
            else:
                eng.wait_ge(kt_done, kt_value(l, last_kt))

        def lay(prefix, *parts):
            return [f"{prefix}{p}" for p in parts]

        S_PE = Steps(sem("setup_pe"), [f"hT{k}" for k in range(KT)] + ["small", "ba", "dec"] +
                     [f"yT{k}" for k in range(KT)])
        S_ACT = Steps(sem("setup_act"), ["sq0", "sq1", "sq2", "sq3", "ln", "r"] + [f"hi{k}" for k in range(KT)] +
                      ["smT", "ba", "eb", "aab", "ea", "la", "A", "decs"] + [f"yhi{k}" for k in range(KT)])
        S_DVE = Steps(sem("setup_dve"), ["pc", "pr", "lam"] + [f"x{t}" for t in T] +
                      [f"lo{k}" for k in range(KT)] +
                      ["b1", "beta", "nbeta", "av", "sp", "glog", "gA", "zero_gdn"] +
                      [f"ylo{k}" for k in range(KT)])
        CONV_DVE = Steps(sem("conv_dve"), [f"{c}{b}{s}" for c in ("dq", "dk", "dv") for b in range(4)
                                           for s in ("t3", "t2", "t1", "t0", "one", "rec", "mul")])
        CONV_ACT = Steps(sem("conv_act"), [f"{c}{b}" for c in ("dq", "dk", "dv") for b in range(4)])
        D_PE = Steps(sem("gdn_pe"), names("", T, GDN_PE))
        D_ACT = Steps(sem("gdn_act"), names("", T, GDN_ACT))
        D_DVE = Steps(sem("gdn_dve"), names("", T, GDN_DVE))
        A_PE = Steps(sem("gla_pe"), names("", T, GLA_PE))
        A_ACT = Steps(sem("gla_act"), names("", T, GLA_ACT))
        A_DVE = Steps(sem("gla_dve"), ["zero_s", "zero_a"] + names("", T, GLA_DVE))
        B_PE = Steps(sem("swa_pe"), names("", T, SWA_PE))
        B_ACT = Steps(sem("swa_act"), names("", T, SWA_ACT))
        B_DVE = Steps(sem("swa_dve"), names("", T, SWA_DVE))
        R_PE = Steps(sem("prep_pe"), names("", T, PREP_PE))
        R_ACT = Steps(sem("prep_act"), names("", T, PREP_ACT))
        N_ACT = Steps(sem("norm_act"), names("", T, NORM_ACT))
        N_DVE = Steps(sem("norm_dve"), names("", T, NORM_DVE))
        back = list(reversed(T))
        C_PE = Steps(sem("dif_pe"), names("", back, DIF_PE))
        C_ACT = Steps(sem("dif_act"), names("", back, DIF_ACT))
        C_DVE = Steps(sem("dif_dve"), names("", back, DIF_DVE))

        block = ctx.enter_context(nc.Block())

        @block.sync
        def _(sp):
            for l in range(DEPTH):
                sp.dma_start(prow_all[:, l], prow[l, 0:12].partition_broadcast(P)).then_inc(params_in, 16)
                sp.dma_start(slot(4)[:, l, 0:NPR], prow[l].partition_broadcast(P)).then_inc(params_in, 16)
            sp.dma_start(pcol_all[:, :, :], pcol.rearrange("l p n -> p l n")).then_inc(params_in, 16)
            for t in T:
                sp.dma_start(xf[:, t], x[t * P:(t + 1) * P, :]).then_inc(xin[t], 16)
            sp.dma_start(cf_sb[:, :], cf).then_inc(consts_in, 16)
            sp.dma_start(slot(10).rearrange("p a b -> p (a b)")[:, 0:masks.shape[1]], masks).then_inc(masks_in, 16)
            with sp.Fori(0, DEPTH) as l:
                sp.wait_ge(ws_ready, l + 1)
                sp.dma_start(ws_raw[:, :], wsmall[bass.ds(l, 1)].rearrange("a p n -> p (a n)")).then_inc(ws_in, 16)
                with sp.Fori(0, PAIRS // RAW) as i:
                    for s in range(RAW):
                        sp.wait_ge(raw_used, l * PAIRS + i * RAW + (s + 1))
                        sp.dma_start(w_raw[:, s].rearrange("p a n -> p (a n)"),
                                     wstream[bass.ds(l * PAIRS + i * RAW + s, 1)].rearrange("a p n -> p (a n)")
                                     ).then_inc(raw_in[s], 16)

        @block.gpsimd
        def _(pool):
            pool.sem_inc(raw_used, RAW)
            pool.sem_inc(ws_ready, 1)
            pool.memset(zeros[:, :], 0.0).then_inc(zeros_done, 1)
            pool.wait_ge(zeros_done, 1)
            pool.memset(ws_hi[:, KT * NSM:].bitcast(F32), 0.0).then_inc(zeros_done, 1)
            pool.memset(ws_lo[:, KT * NSM:].bitcast(F32), 0.0).then_inc(zeros_done, 1)
            pool.wait_ge(masks_in, 16)
            pool.wait_ge(consts_in, 16)
            pool.tensor_copy(mask_sb[:, 0:masks.shape[1]], slot(10).rearrange("p a b -> p (a b)")
                             [:, 0:masks.shape[1]]).then_inc(masks_done, 1)
            pool.tensor_copy(m_upto, upto).then_inc(masks_done, 1)
            for s in range(RAW):
                pool.wait_ge(raw_in[s], 16)
            pool.dma_start(out[:, :], x[:, :]).then_inc(xcopy, 16)
            with pool.Fori(0, DEPTH) as l:
                pool.wait_ge(ws_in, l * 16 + 16)
                pool.wait_ge(kt_done, l * LAYER_KTS + RING)
                pool.tensor_tensor(ws_hi[:, 0:KT * NSM], ws_raw[:, :],
                                   zeros[:, :].broadcast_to([P, KT * NSM]), ALU.add).then_inc(ws_hi_done, 1)
                pool.wait_ge(ws_hi_done, l + 1)
                pool.tensor_tensor(ws_lo[:, 0:KT * NSM], ws_raw[:, :], ws_hi[:, 0:KT * NSM].bitcast(F32),
                                   ALU.subtract).then_inc(ws_ready, 1)
                with pool.Fori(0, PAIRS // RAW) as i:
                    for s in range(RAW):
                        pool.wait_ge(raw_in[s], l * (16 * PAIRS // RAW) + i * 16 + 16)
                        for k in range(2):
                            n, r = 2 * s + k, (2 * s + k) % RING
                            pool.wait_ge(kt_done, l * LAYER_KTS + i * (2 * RAW) + (n + 1))
                            pool.tensor_tensor(w_hi[:, r], w_raw[:, s, k], zeros[:, :].broadcast_to([P, GW]), ALU.add).then_inc(hi_done, 1)
                            pool.wait_ge(hi_done, l * LAYER_KTS + i * (2 * RAW) + (n + 1))
                            pool.tensor_tensor(w_lo[:, r], w_raw[:, s, k], w_hi[:, r].bitcast(F32),
                                               ALU.subtract).then_inc(w_ready, 1)
                        pool.wait_ge(w_ready, l * LAYER_KTS + i * (2 * RAW) + (2 * s + 2))
                        pool.sem_inc(raw_used, 1)

        @block.tensor
        def _(pe):
            pe.sem_inc(kt_done, RING)

            def plain():
                pe.sem_inc(pe_passed, 1)

            def project(l, q, kt0, kts, act_kt, turned=False, ahead=None, mixer=None, stages=1, skip=0,
                        spread=1.0):
                slots_n, given = int(spread * 2 * (kts - skip)), 0
                for k in range(kts):
                    if ahead:
                        ahead(k)
                    r = (kt0 + k) % RING
                    pe.wait_ge(w_ready, l * LAYER_KTS + (kt0 + k + 1))
                    for b in range(4):
                        if k == 0:
                            pe.wait_ge(acc_free, acc_free_value(l, q, b))
                        c = slice(b * P, b * P + P)
                        a = act_kt + k
                        if turned:
                            terms = [(w_hi[:, r, c], actT_hi[:, a]), (w_hi[:, r, c], actT_lo[:, a]),
                                     (w_lo[:, r, c], actT_hi[:, a])]
                        else:
                            terms = [(actT_hi[:, a, c], w_hi[:, r]), (actT_hi[:, a, c], w_lo[:, r]),
                                     (actT_lo[:, a, c], w_hi[:, r])]
                        for i, (lhsT, rhs) in enumerate(terms):
                            last = nc.tensor.matmul(acc[b][:, :], lhsT, rhs, start=(k == 0 and i == 0),
                                                    stop=(k == kts - 1 and i == 2))
                        if b == 3:
                            last.then_inc(kt_done, 1)
                        elif k == kts - 1:
                            last.then_inc(acc_ready, 1)
                        if mixer and b % 2 and k >= skip:
                            n = 2 * (k - skip) + b // 2 + 1
                            while given * slots_n < n * stages and given < stages:
                                next(mixer, None)
                                given += 1
                if mixer:
                    for _ in mixer:
                        pass

            def gdn(l, t):
                cs = slice(t * P, t * P + P)
                q, k, v = (slot(CONV[c]) for c in ("dq", "dk", "dv"))
                QN, KN, QD, KB, KE, VN = U["QN"], U["KN"], U["QD"], U["KB"], U["KE"], U["VN"]
                yield
                if t:
                    pe.wait_ge(D_DVE.sem, D_DVE.at(l, f"{t-1}.y3"))
                else:
                    pe.wait_ge(S_ACT.sem, S_ACT.at(l, "decs"))
                    pe.wait_ge(CONV_DVE.sem, CONV_DVE.at(l, "dv3mul"))
                pe.wait_ge(D_DVE.sem, D_DVE.at(l, f"{t}.ag"))
                for h in H:
                    last = nc.tensor.matmul(mh[3][:, h], U["AG"][:, h], upto, start=True, stop=True)
                last.then_inc(D_PE.sem, D_PE.one(f"{t}.gap"))
                for i, s in enumerate((q, k, v)):
                    for h in H:
                        last = nc.tensor.transpose(mh[i][:, h], s[:, h, cs], ident)
                last.then_inc(D_PE.sem, D_PE.one(f"{t}.nat"))
                yield
                yield
                yield
                yield
                pe.wait_ge(D_DVE.sem, D_DVE.at(l, f"{t}.qd"))
                pe.wait_ge(D_ACT.sem, D_ACT.at(l, f"{t}.vn"))
                for i, s in enumerate((QN, KN, QD)):
                    for h in H:
                        last = nc.tensor.transpose(mh[i][:, h], s[:, h], ident)
                last.then_inc(D_PE.sem, D_PE.one(f"{t}.back"))
                yield
                pe.wait_ge(D_ACT.sem, D_ACT.at(l, f"{t}.kT"))
                for h in H:
                    last = nc.tensor.matmul(mh[0][:, h], U["KT"][:, h], U["KT"][:, h], start=True, stop=True)
                last.then_inc(D_PE.sem, D_PE.one(f"{t}.kk"))
                for h in H:
                    last = nc.tensor.matmul(mh[1][:, h], U["KT"][:, h], U["QT"][:, h], start=True, stop=True)
                last.then_inc(D_PE.sem, D_PE.one(f"{t}.kq"))
                yield
                pe.wait_ge(D_DVE.sem, D_DVE.at(l, f"{t}.mt"))
                for h in H:
                    last = nc.tensor.transpose(mh[2][:, h], U["MT"][:, h], ident)
                last.then_inc(D_PE.sem, D_PE.one(f"{t}.m1"))
                yield
                for lv in range(2, LEVELS + 1):
                    pe.wait_ge(D_DVE.sem, D_DVE.at(l, f"{t}.x{lv-1}"))
                    for h in H:
                        last = nc.tensor.matmul(mh[3][:, h], U["MT"][:, h], U["X"][:, h], start=True, stop=True)
                    last.then_inc(D_PE.sem, D_PE.one(f"{t}.y{lv}"))
                    for h in H:
                        last = nc.tensor.transpose(mh[1][:, h], U["X"][:, h], ident)
                    last.then_inc(D_PE.sem, D_PE.one(f"{t}.tx{lv}"))
                    yield
                    pe.wait_ge(D_ACT.sem, D_ACT.at(l, f"{t}.y{lv}"))
                    pe.wait_ge(D_DVE.sem, D_DVE.at(l, f"{t}.xt{lv}"))
                    for h in H:
                        if lv < LEVELS:
                            last = nc.tensor.matmul(mh[0][:, h], U["XT"][:, h], U["Y"][:, h], start=True, stop=True)
                        else:
                            last = nc.tensor.matmul(mh[0][:, h], U["Y"][:, h], U["XT"][:, h], start=True, stop=True)
                    last.then_inc(D_PE.sem, D_PE.one(f"{t}.{'p' if lv < LEVELS else 'pt'}{lv}"))
                    yield
                pe.wait_ge(D_DVE.sem, D_DVE.at(l, f"{t}.xt7"))
                for h in H:
                    last = nc.tensor.matmul(mh[2][:, h], KB[:, h], U["XT"][:, h], start=True, stop=True)
                last.then_inc(D_PE.sem, D_PE.one(f"{t}.w"))
                for h in H:
                    last = nc.tensor.matmul(mh[1][:, h], U["XT"][:, h], VN[:, h], start=True, stop=True)
                last.then_inc(D_PE.sem, D_PE.one(f"{t}.u"))
                yield
                for j in range(2):
                    r = slice(CH * j, CH * j + CH)
                    S = U["S"][j]
                    pe.wait_ge(D_ACT.sem, D_ACT.at(l, f"{t}.wT"))
                    if j:
                        pe.wait_ge(D_DVE.sem, D_DVE.at(l, f"{t}.s03"))
                    for h in H:
                        last = nc.tensor.matmul(mh[3][r, h], U["WT"][:, h, r], S[:, h], start=True, stop=True)
                    last.then_inc(D_PE.sem, D_PE.one(f"{t}.v{j}"))
                    yield
                    yield
                    pe.wait_ge(D_DVE.sem, D_DVE.at(l, f"{t}.v{j}3"))
                    for h in H:
                        last = nc.tensor.matmul(mh[j][:, h], KE[r, h], U["VW"][r, h], start=True, stop=True)
                    last.then_inc(D_PE.sem, D_PE.one(f"{t}.s{j}"))
                    if j == 0:
                        yield
                for h in H:
                    nc.tensor.matmul(mh[2][:, h], U["QK"][:, h], U["VW"][:, h], start=True, stop=False)
                    for j in range(2):
                        r = slice(CH * j, CH * j + CH)
                        last = nc.tensor.matmul(mh[2][r, h], U["QDT"][:, h, r], U["S"][j][:, h],
                                                start=False, stop=True)
                last.then_inc(D_PE.sem, D_PE.one(f"{t}.o"))
                yield

            def gla(l, t):
                yield
                if t:
                    pe.wait_ge(A_DVE.sem, A_DVE.at(l, f"{t-1}.y3"))
                else:
                    pe.wait_ge(D_DVE.sem, D_DVE.at(l, f"{TILES-1}.y3"))
                pe.wait_ge(wlr_in, l * 16 + 16)
                nc.tensor.matmul(mix[1][:, 0:256], smT[:, t * P:t * P + P], wlr_sb[:, :],
                                 start=True, stop=True).then_inc(A_PE.sem, A_PE.one(f"{t}.u"))
                yield
                pe.wait_ge(A_DVE.sem, A_DVE.at(l, f"{t}.g"))
                nc.tensor.matmul(mix[0][:, 0:256], upto, V["G"], start=True, stop=True)
                nc.tensor.matmul(mix[0][:, 256:512], after, V["G"], start=True, stop=True) \
                    .then_inc(A_PE.sem, A_PE.one(f"{t}.cum"))
                for p in range(2):
                    for j in range(2):
                        last = nc.tensor.matmul(mix[1][:, 2 * p + j:2 * p + j + 1], V["G"][:, p * P:p * P + P],
                                                half[j][:, 0:1], start=True, stop=True)
                last.then_inc(A_PE.sem, A_PE.one(f"{t}.dec"))
                yield
                pe.wait_ge(A_DVE.sem, A_DVE.at(l, f"{t}.ki"))
                for i, s in enumerate((V["QD"], V["KI"])):
                    for p in range(2):
                        last = nc.tensor.transpose(mix[2][:, 256 * i + P * p:256 * i + P * p + P],
                                                   s[:, p * P:p * P + P], ident)
                last.then_inc(A_PE.sem, A_PE.one(f"{t}.tr"))
                yield
                pe.wait_ge(A_ACT.sem, A_ACT.at(l, f"{t}.qkT"))
                for h in H:
                    b, p = slice(DK * (h % 2), DK * (h % 2) + DK), h // 2
                    last = nc.tensor.matmul(mh[3 - h % 2][:, h], V["QKT"][b, 256 + P * p:256 + P * p + P],
                                            V["QKT"][b, P * p:P * p + P], start=True, stop=True)
                last.then_inc(A_PE.sem, A_PE.one(f"{t}.a"))
                pe.wait_ge(A_DVE.sem, A_DVE.at(l, f"{t}.ke"))
                pe.wait_ge(A_ACT.sem, A_ACT.at(l, f"{t}.dect"))
                plain()
                for h in H:
                    for j in range(2):
                        r = slice(CH * j, CH * j + CH)
                        o = slice(DK * (h % 2), DK * (h % 2) + DK)
                        last = nc.tensor.matmul(mh[j][o, h // 2], V["KE"][r, DK * h:DK * h + DK],
                                                slot(SLOT["av"])[r, t, HD * h:HD * h + HD], start=True, stop=True)
                last.then_inc(A_PE.sem, A_PE.one(f"{t}.us"))
                yield
                pe.wait_ge(A_DVE.sem, A_DVE.at(l, f"{t}.s11"))
                for h in H:
                    b, p = slice(DK * (h % 2), DK * (h % 2) + DK), h // 2
                    o = mh[3 if h % 2 else 1]
                    nc.tensor.matmul(o[:, h], V["AT"][:, h], slot(SLOT["av"])[:, t, HD * h:HD * h + HD],
                                     start=True, stop=False)
                    for j in range(2):
                        r = slice(CH * j, CH * j + CH)
                        last = nc.tensor.matmul(o[r, h], V["QKT"][b, P * p + CH * j:P * p + CH * j + CH],
                                                V["S"][b, (2 * t + j) % 3, p], start=False, stop=True)
                last.then_inc(A_PE.sem, A_PE.one(f"{t}.o"))
                yield

            def swa(l, t):
                q, kv = slot(SLOT["bq"]), slot(SLOT["bkv"])
                yield
                if t:
                    pe.wait_ge(B_ACT.sem, B_ACT.at(l, f"{t-1}.PT0"))
                    pe.wait_ge(B_DVE.sem, B_DVE.at(l, f"{t-1}.PT1"))
                else:
                    pe.wait_ge(A_DVE.sem, A_DVE.at(l, f"{TILES-1}.y3"))
                pe.wait_ge(N_DVE.sem, N_DVE.at(l, f"{t}.bk"))
                for h in H:
                    nc.tensor.transpose(mh[0][:, h], q[:, t, h * HD:h * HD + HD], ident)
                for g in range(2):
                    last = nc.tensor.transpose(mh[1][:, g], kv[:, t, g * HD:g * HD + HD], ident)
                last.then_inc(B_PE.sem, B_PE.one(f"{t}.tr"))
                yield
                pe.wait_ge(B_ACT.sem, B_ACT.at(l, f"{t}.kT"))
                if t:
                    pe.wait_ge(B_DVE.sem, B_DVE.at(l, f"{t-1}.y3"))
                n = min(t, 1) + 1
                for h in H:
                    last = nc.tensor.matmul(mix[2 + h // 2][:, 256 * (h % 2):256 * (h % 2) + P * n], W["QT"][:, h],
                                            kv[:, t + 1 - n:t + 1, (h // 2) * HD:(h // 2) * HD + HD],
                                            start=True, stop=True)
                    if h % 2:
                        last.then_inc(B_PE.sem, B_PE.one(f"{t}.s{h//2}"))
                yield
                pe.wait_ge(N_DVE.sem, N_DVE.at(l, f"{t}.ck"))
                for i, c in enumerate(("cq", "ck")):
                    for h in H:
                        last = nc.tensor.transpose(mh[i][:, h], slot(SLOT[c])[:, t, h * HD:h * HD + HD], ident)
                    last.then_inc(R_PE.sem, R_PE.one(f"{t}.{'qk'[i]}"))
                yield
                yield
                pe.wait_ge(R_ACT.sem, R_ACT.at(l, f"{t}.kT"))
                for i in range(2):
                    pe.wait_ge(B_ACT.sem, B_ACT.at(l, f"{t}.p{2*i+1}"))
                    for h in (2 * i, 2 * i + 1):
                        for m in range(n):
                            last = nc.tensor.transpose(mix[i][:, 256 * (h % 2) + P * m:256 * (h % 2) + P * m + P],
                                                       W["SB"][:, h, P * m:P * m + P], ident)
                    last.then_inc(B_PE.sem, B_PE.one(f"{t}.pt{i}"))
                yield
                pe.wait_ge(B_ACT.sem, B_ACT.at(l, f"{t}.PT0"))
                pe.wait_ge(B_DVE.sem, B_DVE.at(l, f"{t}.PT1"))
                for h in H:
                    for m in range(n):
                        last = nc.tensor.matmul(mh[2][:, h], W["PT"][:, h, P * m:P * m + P],
                                                kv[:, t + 1 - n + m, 256 + (h // 2) * HD:256 + (h // 2) * HD + HD],
                                                start=(m == 0), stop=(m == n - 1))
                last.then_inc(B_PE.sem, B_PE.one(f"{t}.pv"))
                yield

            def dif(l, t):
                n = t + 1
                qT, kT, v = (slot(SLOT[c]) for c in ("cq", "ck", "cv"))

                def scores(h):
                    if h:
                        pe.wait_ge(C_DVE.sem, C_DVE.at(l, f"{t}.b{h-1}1"))
                    elif t < TILES - 1:
                        pe.wait_ge(C_DVE.sem, C_DVE.at(l, f"{t+1}.b{HEADS-1}1"))
                    else:
                        pe.wait_ge(S_DVE.sem, S_DVE.at(l, f"ylo{3*HEADS-1}"))
                    for m in range(2):
                        r = slice(DK * m, DK * m + DK)
                        last = nc.tensor.matmul(mix[m][:, 0:P * n], qT[r, t, HD * h:HD * h + HD],
                                                kT[r, 0:n, HD * h:HD * h + HD], start=True, stop=True)
                    last.then_inc(C_PE.sem, C_PE.one(f"{t}.s{h}"))

                def turn(h):
                    pe.wait_ge(C_DVE.sem, C_DVE.at(l, f"{t}.w{h}"))
                    if h:
                        pe.wait_ge(C_ACT.sem, C_ACT.at(l, f"{t}.wT{h-1}"))
                    for j in range(n):
                        last = nc.tensor.transpose(mh[2][:, j], Z["S"][h % 2][0][:, P * j:P * j + P], ident)
                    last.then_inc(C_PE.sem, C_PE.one(f"{t}.t{h}"))

                def values(h):
                    pe.wait_ge(C_ACT.sem, C_ACT.at(l, f"{t}.wT{h}"))
                    if h == 0 and t < TILES - 1:
                        pe.wait_ge(C_DVE.sem, C_DVE.at(l, f"{t+1}.os"))
                    for j in range(n):
                        last = nc.tensor.matmul(mh[3][:, h], Z["WT"][h % 2][:, j], v[:, j, HD * h:HD * h + HD],
                                                start=(j == 0), stop=(j == n - 1))
                    last.then_inc(C_PE.sem, C_PE.one(f"{t}.v{h}"))

                scores(0)
                yield
                scores(1)
                yield
                yield
                for h in H:
                    turn(h)
                    yield
                    values(h)
                    yield
                    if h + 2 < HEADS:
                        scores(h + 2)
                        yield

            def turn_x(l, k):
                if k >= 4:
                    pe.wait_ge(S_DVE.sem, S_DVE.at(l, f"lo{k-4}"))
                for t in T:
                    last = nc.tensor.transpose(mh[k % 4][:, t], xf[:, t, k * P:k * P + P], ident)
                last.then_inc(S_PE.sem, S_PE.one(f"hT{k}"))

            def turn_y(l, k):
                src = slot(SLOT[("dz", "az", "bz", "cz")[k // 4]])
                if k == 0:
                    pe.wait_ge(B_DVE.sem, B_DVE.at(l, f"{TILES-1}.y3"))
                    pe.wait_ge(R_ACT.sem, R_ACT.at(l, f"{TILES-1}.kT"))
                elif k == 3 * HEADS:
                    pe.wait_ge(C_DVE.sem, C_DVE.at(l, "0.y3"))
                elif k >= 4:
                    pe.wait_ge(S_DVE.sem, S_DVE.at(l, f"ylo{k-4}"))
                for t in T:
                    last = nc.tensor.transpose(mh[k % 4][:, t], src[:, t, (k % 4) * P:(k % 4) * P + P], ident)
                last.then_inc(S_PE.sem, S_PE.one(f"yT{k}"))

            pe.wait_ge(consts_in, 16)
            pe.wait_ge(ones_done, 1)
            pe.wait_ge(zeros_done, 3)
            with pe.Fori(0, DEPTH) as l:
                pe.wait_ge(S_DVE.sem, S_DVE.at(l, "x3"))
                for k in range(4):
                    turn_x(l, k)

                def h_ready(k):
                    pe.wait_ge(S_DVE.sem, S_DVE.at(l, f"lo{k}"))
                    if k + 4 < KT:
                        turn_x(l, k + 4)

                project(l, 0, 0, KT, 0, turned=True, ahead=h_ready)
                pe.wait_ge(ws_ready, l + 2)
                for k in range(KT):
                    c = slice(k * NSM, k * NSM + P)
                    for i, (a, w) in enumerate(((actT_hi, ws_hi), (actT_lo, ws_hi), (actT_hi, ws_lo))):
                        last = nc.tensor.matmul(mix[0][:, :], w[:, c], a[:, k], start=(k == 0 and i == 0),
                                                stop=(k == KT - 1 and i == 2))
                last.then_inc(S_PE.sem, S_PE.one("small"))
                pe.wait_ge(S_ACT.sem, S_ACT.at(l, "smT"))
                plain()
                for t in T:
                    last = nc.tensor.transpose(mix[1][:, 32 * t:32 * t + NSM], smT[0:NSM, t * P:t * P + P],
                                               ident[0:NSM, 0:NSM])
                last.then_inc(S_PE.sem, S_PE.one("ba"))
                project(l, 1, KT, KT, 0, turned=True)
                pe.wait_ge(S_DVE.sem, S_DVE.at(l, "gA"))
                gl = glog[:, :, :].rearrange("p t h -> p (t h)")
                for i, w in enumerate((upto, after, half[0], half[1])):
                    last = nc.tensor.matmul(mix[3][:, 16 * i:16 * i + 16], w, gl, start=True, stop=True)
                last.then_inc(S_PE.sem, S_PE.one("dec"))
                project(l, 2, 2 * KT, KT, 0, turned=True)
                project(l, 3, 3 * KT, KT, 0)
                for t in T:
                    project(l, 4 + t, (4 + t) * KT, KT, 0, mixer=gdn(l, t), stages=25, skip=1, spread=1.0)
                for t in T:
                    project(l, 8 + t, (8 + t) * KT, KT, 0, mixer=gla(l, t), stages=6, skip=1, spread=0.75)
                for i in range(2):
                    def both(l=l, i=i):
                        for t in (2 * i, 2 * i + 1):
                            yield from swa(l, t)
                    project(l, 12 + i, (12 + i) * KT, KT, 0, mixer=both(), stages=14, skip=(2, 0)[i],
                            spread=(0.95, 0.85)[i])
                for k in range(4):
                    turn_y(l, k)
                for n in T:
                    def y_ready(k, n=n):
                        if n == 0:
                            pe.wait_ge(S_DVE.sem, S_DVE.at(l, f"ylo{k}"))
                            for m in (4 + 2 * k, 5 + 2 * k):
                                if m < 3 * HEADS:
                                    turn_y(l, m)
                    project(l, 14 + n, IN_KTS + 12 * n, 12, 0, ahead=y_ready, mixer=dif(l, TILES - 1 - n),
                            stages=13, skip=(4 if n == 0 else 0), spread=(1.0, 0.8, 0.7, 0.6)[n])
                for k in range(12, 16):
                    turn_y(l, k)
                for n in T:
                    def c_ready(k, n=n):
                        if n == 0:
                            pe.wait_ge(S_DVE.sem, S_DVE.at(l, f"ylo{12+k}"))
                    project(l, 18 + n, IN_KTS + OUT_KTS + 4 * n, 4, 12, ahead=c_ready)

        @block.scalar
        def _(act):
            act.sem_inc(acc_free, 4)
            act.sem_inc(xout, 1)

            def take_out(l, c):
                q = CHUNKS.index(c)
                for b in range(4):
                    wait_acc(act, l, q, b, q * KT + KT - 1)
                    nc.scalar.activation(slot(SLOT[c])[:, b], acc[b][:, :], ACT.Copy).then_inc(acc_free, 1)

            def rms(l, St, t, ln, r, src, dst, scale, ready):
                ready()
                nc.scalar.activation(dst, src, ACT.Ln, bias=eps_t[:, :], scale=scale).then_inc(St.sem, St.one(ln))
                act.wait_ge(St.sem, St.at(l, ln))
                nc.scalar.activation(dst, dst, ACT.Exp, scale=-0.5).then_inc(St.sem, St.one(r))

            act.wait_ge(lam_steps, 2 * DEPTH)
            nc.scalar.activation(stat[:, 32:32 + 2 * DEPTH], stat[:, 0:2 * DEPTH], ACT.Exp).then_inc(lam_act, 1)
            act.wait_ge(lam_act, 1)

            with act.Fori(0, DEPTH) as l:
                act.wait_ge(acc_free, l * (4 * N_ACC) + 4)
                for t in T:
                    act.wait_ge(xin[t], 16)
                    if t >= 2:
                        act.wait_ge(S_ACT.sem, S_ACT.at(l, f"sq{t-2}"))
                    nc.scalar.activation(slot((5, 13)[t % 2]).rearrange("p a b -> p (a b)"), xf[:, t], ACT.Square,
                                         accum_out=ss[:, t:t + 1]).then_inc(S_ACT.sem, S_ACT.one(f"sq{t}"))
                act.wait_ge(S_ACT.sem, S_ACT.at(l, "sq3"))
                nc.scalar.activation(rs[:, 0:4], ss[:, 0:4], ACT.Ln, bias=eps_t[:, :],
                                     scale=1.0 / D_MODEL).then_inc(S_ACT.sem, S_ACT.one("ln"))
                act.wait_ge(S_ACT.sem, S_ACT.at(l, "ln"))
                nc.scalar.activation(rs[:, 0:4], rs[:, 0:4], ACT.Exp, scale=-0.5).then_inc(S_ACT.sem, S_ACT.one("r"))
                act.dma_start(wlr_sb[:, :], wlr[bass.ds(l, 1)].rearrange("a r n -> (a r) n")).then_inc(wlr_in, 16)
                act.wait_ge(S_DVE.sem, S_DVE.at(l, "pc"))
                for k in range(KT):
                    act.wait_ge(S_PE.sem, S_PE.at(l, f"hT{k}"))
                    nc.scalar.activation(actT_hi[:, k], mix[k % 4][:, :], ACT.Copy,
                                         scale=pc[:, PC["norm"] + k:PC["norm"] + k + 1]) \
                        .then_inc(S_ACT.sem, S_ACT.one(f"hi{k}"))

                def conv_gate(c):
                    for b in range(4):
                        act.wait_ge(CONV_DVE.sem, CONV_DVE.at(l, f"{c}{b}t0"))
                        if b >= 2:
                            act.wait_ge(CONV_DVE.sem, CONV_DVE.at(l, f"{c}{b-2}mul"))
                        nc.scalar.activation(general[:, b % 2], slot(CONV[c])[:, b], ACT.Exp, scale=-1.0) \
                            .then_inc(CONV_ACT.sem, CONV_ACT.one(f"{c}{b}"))

                act.wait_ge(S_PE.sem, S_PE.at(l, "small"))
                nc.scalar.activation(smT[0:NSM, :], mix[0][0:NSM, :], ACT.Copy).then_inc(S_ACT.sem, S_ACT.one("smT"))
                take_out(l, "dq")
                act.wait_ge(S_PE.sem, S_PE.at(l, "ba"))
                sm = mix[1][:, 0:128].rearrange("p (t c) -> p t c", t=TILES)
                nc.scalar.activation(small[:, :, :], sm[:, :, RANK:NSM], ACT.Copy).then_inc(S_ACT.sem, S_ACT.one("ba"))
                act.wait_ge(S_ACT.sem, S_ACT.at(l, "ba"))
                nc.scalar.activation(beta[:, :, :], small[:, :, 0:HEADS], ACT.Exp, scale=-1.0) \
                    .then_inc(S_ACT.sem, S_ACT.one("eb"))
                act.wait_ge(S_DVE.sem, S_DVE.at(l, "av"))
                t16 = stat[:, 0:16].rearrange("p (t h) -> p t h", t=TILES)
                nc.scalar.activation(t16, small[:, :, HEADS:], ACT.Abs) \
                    .then_inc(S_ACT.sem, S_ACT.one("aab"))
                act.wait_ge(S_ACT.sem, S_ACT.at(l, "aab"))
                nc.scalar.activation(t16, t16, ACT.Exp, scale=-1.0).then_inc(S_ACT.sem, S_ACT.one("ea"))
                act.wait_ge(S_ACT.sem, S_ACT.at(l, "ea"))
                nc.scalar.activation(t16, t16, ACT.Ln, bias=1.0).then_inc(S_ACT.sem, S_ACT.one("la"))
                nc.scalar.activation(sa, pr[:, PR["alog"]:PR["alog"] + 4], ACT.Exp) \
                    .then_inc(S_ACT.sem, S_ACT.one("A"))
                conv_gate("dq")
                take_out(l, "dk")
                act.wait_ge(S_PE.sem, S_PE.at(l, "dec"))
                nc.scalar.activation(decs[:, :, :, :].rearrange("p a t h -> p (a t h)"), mix[3][:, 0:64], ACT.Exp) \
                    .then_inc(S_ACT.sem, S_ACT.one("decs"))
                conv_gate("dk")
                take_out(l, "dv")
                conv_gate("dv")
                take_out(l, "dz")

                def gate(St, step, src, dst, free=None):
                    nc.scalar.activation(dst, src, ACT.Exp, scale=-1.0).then_inc(St.sem, St.one(step))

                for t in T:
                    A, VE, PE_ = D_ACT, D_DVE, D_PE
                    w = lambda st, s, t=t: act.wait_ge(st.sem, st.at(l, f"{t}.{s}"))
                    s = lambda step, t=t: (D_ACT.sem, D_ACT.one(f"{t}.{step}"))
                    w(D_PE, "nat")
                    nc.scalar.activation(U["SQ"][:, 0:4], mh[0], ACT.Square).then_inc(*s("sqq"))
                    nc.scalar.activation(U["SQ"][:, 4:8], mh[1], ACT.Square).then_inc(*s("sqk"))
                    w(D_DVE, "red")
                    nc.scalar.activation(rs[:, 0:8], ss[:, 0:8], ACT.Ln, bias=eps_t[:, :]).then_inc(*s("lnr"))
                    w(D_ACT, "lnr")
                    nc.scalar.activation(rs[:, 0:8], rs[:, 0:8], ACT.Exp, scale=-0.5).then_inc(*s("rr"))
                    nc.scalar.activation(U["VN"], mh[2], ACT.Copy).then_inc(*s("vn"))
                    w(D_PE, "gap")
                    nc.scalar.activation(U["EX"], mh[3], ACT.Exp).then_inc(*s("ex"))
                    w(D_PE, "back")
                    nc.scalar.activation(U["QT"], mh[0], ACT.Copy, scale=HD ** -0.5).then_inc(*s("qT"))
                    nc.scalar.activation(U["QDT"], mh[2], ACT.Copy, scale=HD ** -0.5).then_inc(*s("qdT"))
                    w(D_DVE, "ke")
                    nc.scalar.activation(U["KT"], mh[1], ACT.Copy).then_inc(*s("kT"))
                    for lv in range(2, LEVELS + 1):
                        w(D_PE, f"y{lv}")
                        nc.scalar.activation(U["Y"], mh[3], ACT.Copy).then_inc(*s(f"y{lv}"))
                    w(D_PE, "w")
                    nc.scalar.activation(U["WT"], mh[2], ACT.Copy, scale=-1.0).then_inc(*s("wT"))
                    gz = slot(SLOT["dz"])[:, t].rearrange("p (h c) -> p h c", h=HEADS)
                    if t == 0:
                        act.wait_ge(acc_free, acc_free_after(l, CHUNKS.index("dz"), 3))
                    nc.scalar.activation(U["GATE"], gz, ACT.Exp, scale=-1.0).then_inc(*s("gate"))
                    take_out(l, CHUNKS[4 + t])
                    w(D_PE, "o")
                    nc.scalar.activation(U["SQO"], mh[2], ACT.Square).then_inc(*s("sqo"))
                    w(D_DVE, "redo")
                    nc.scalar.activation(sa, ss[:, 0:4], ACT.Ln, bias=eps_t[:, :], scale=1.0 / HD) \
                        .then_inc(*s("lno"))
                    w(D_ACT, "lno")
                    nc.scalar.activation(sa, sa, ACT.Exp, scale=-0.5).then_inc(*s("ro"))

                for t in T:
                    w = lambda st, s, t=t: act.wait_ge(st.sem, st.at(l, f"{t}.{s}"))
                    s = lambda step, t=t: (A_ACT.sem, A_ACT.one(f"{t}.{step}"))
                    w(A_PE, "u")
                    nc.scalar.activation(V["T0"], mix[1][:, 0:256], ACT.Abs).then_inc(*s("abs"))
                    w(A_ACT, "abs")
                    nc.scalar.activation(V["T0"], V["T0"], ACT.Exp, scale=-1.0).then_inc(*s("e"))
                    w(A_ACT, "e")
                    nc.scalar.activation(V["T0"], V["T0"], ACT.Ln, bias=1.0).then_inc(*s("l"))
                    w(A_PE, "cum")
                    nc.scalar.activation(V["EB"], mix[0][:, 0:256], ACT.Exp, scale=1.0 / 16).then_inc(*s("eb"))
                    nc.scalar.activation(V["ENB"], mix[0][:, 0:256], ACT.Exp, scale=-1.0 / 16).then_inc(*s("enb"))
                    nc.scalar.activation(V["ER"], mix[0][:, 256:512], ACT.Exp, scale=1.0 / 16).then_inc(*s("er"))
                    w(A_PE, "dec")
                    nc.scalar.activation(V["DECT"], mix[1][:, 0:4], ACT.Exp, scale=1.0 / 16).then_inc(*s("dect"))
                    w(A_PE, "tr")
                    nc.scalar.activation(V["QKT"], mix[2][:, :], ACT.Copy).then_inc(*s("qkT"))
                    gz = slot(SLOT["az"])[:, t].rearrange("p (h c) -> p h c", h=HEADS)
                    nc.scalar.activation(V["GATE"], gz, ACT.Exp, scale=-1.0).then_inc(*s("gate"))
                    w(A_PE, "o")
                    for i in range(2):
                        nc.scalar.activation(V["SQO"][:, i::2], mh[1 + 2 * i][:, i::2], ACT.Square) \
                            .then_inc(*s(f"sqo{i}"))
                    w(A_DVE, "redo")
                    nc.scalar.activation(sa, ss[:, 0:4], ACT.Ln, bias=eps_t[:, :], scale=1.0 / HD) \
                        .then_inc(*s("lno"))
                    w(A_ACT, "lno")
                    nc.scalar.activation(sa, sa, ACT.Exp, scale=-0.5).then_inc(*s("ro"))
                    take_out(l, CHUNKS[8 + t])

                def squares(t):
                    s = lambda step: (N_ACT.sem, N_ACT.one(f"{t}.{step}"))
                    if t:
                        act.wait_ge(N_DVE.sem, N_DVE.at(l, f"{t-1}.redc"))
                    nc.scalar.activation(W["SQ"][:, 0:4].rearrange("p g c -> p (g c)"), slot(SLOT["bq"])[:, t],
                                         ACT.Square).then_inc(*s("bq"))
                    nc.scalar.activation(W["SQ"][:, 4:6].rearrange("p g c -> p (g c)"),
                                         slot(SLOT["bkv"])[:, t, 0:256], ACT.Square).then_inc(*s("bk"))
                    for i, c in enumerate(("cq", "ck")):
                        nc.scalar.activation(general[:, i], slot(SLOT[c])[:, t], ACT.Square).then_inc(*s(c))

                def inverses(t):
                    for c, src, dst, width in (("b", ssb, rsb, HD), ("c", ss, rs, DK)):
                        act.wait_ge(N_DVE.sem, N_DVE.at(l, f"{t}.red{c}"))
                        nc.scalar.activation(dst, src, ACT.Ln, bias=eps_t[:, :], scale=1.0 / width) \
                            .then_inc(N_ACT.sem, N_ACT.one(f"{t}.ln{c}"))
                        act.wait_ge(N_ACT.sem, N_ACT.at(l, f"{t}.ln{c}"))
                        nc.scalar.activation(dst, dst, ACT.Exp, scale=-0.5) \
                            .then_inc(N_ACT.sem, N_ACT.one(f"{t}.r{c}"))

                act.wait_ge(acc_free, acc_free_after(l, CHUNKS.index("ck"), 3))
                act.wait_ge(A_DVE.sem, A_DVE.at(l, f"{TILES-1}.y3"))
                squares(0)
                inverses(0)
                for t in T:
                    w = lambda st, s, t=t: act.wait_ge(st.sem, st.at(l, f"{t}.{s}"))
                    s = lambda step, t=t: (B_ACT.sem, B_ACT.one(f"{t}.{step}"))
                    kv = slot(SLOT["bkv"])[:, t]
                    if t:
                        act.wait_ge(B_DVE.sem, B_DVE.at(l, f"{t-1}.g3"))
                    nc.scalar.activation(W["GATE"], slot(SLOT["bz"])[:, t].rearrange("p (h c) -> p h c", h=HEADS),
                                         ACT.Exp, scale=-1.0).then_inc(*s("gate"))
                    w(B_PE, "tr")
                    nc.scalar.activation(W["QT"], mh[0], ACT.Copy, scale=pc[:, PC["gq_b"]:PC["gq_b"] + 1]) \
                        .then_inc(*s("qT"))
                    nc.scalar.activation(kv[:, 0:256], mix[1][:, 0:256], ACT.Copy,
                                         scale=pc[:, PC["gk_b"]:PC["gk_b"] + 1]).then_inc(*s("kT"))
                    if t + 1 < TILES:
                        squares(t + 1)
                    n = P * (min(t, 1) + 1)
                    w(B_DVE, "nm")
                    for h in H:
                        nc.scalar.activation(W["SB"][:, h, 0:n], W["SB"][:, h, 0:n], ACT.Exp, bias=sb2[:, h:h + 1],
                                             accum_out=sc[:, h:h + 1]).then_inc(*s(f"p{h}"))
                    for i, c in enumerate(("q", "k")):
                        w(R_PE, c)
                        g = PC[f"g{c}_c"]
                        nc.scalar.activation(slot(SLOT["c" + c])[:, t], mix[i][:, :], ACT.Copy,
                                             scale=pc[:, g:g + 1]).then_inc(R_ACT.sem, R_ACT.one(f"{t}.{c}T"))
                    w(B_DVE, "es")
                    nc.scalar.activation(sd, sd, ACT.Exp).then_inc(*s("es"))
                    if t + 1 < TILES:
                        inverses(t + 1)
                    w(B_PE, "pt0")
                    nc.scalar.activation(W["PT"][:, 0:2, 0:n],
                                         mix[0][:, :].rearrange("p (h c) -> p h c", h=2)[:, :, 0:n], ACT.Copy) \
                        .then_inc(*s("PT0"))
                    if t % 2:
                        take_out(l, CHUNKS[12 + t // 2])

                def y_hi(k):
                    act.wait_ge(S_PE.sem, S_PE.at(l, f"yT{k}"))
                    nc.scalar.activation(actT_hi[:, k], mix[k % 4][:, :], ACT.Copy,
                                         scale=pc[:, PC["y"] + k:PC["y"] + k + 1]) \
                        .then_inc(S_ACT.sem, S_ACT.one(f"yhi{k}"))

                act.wait_ge(B_DVE.sem, B_DVE.at(l, f"{TILES-1}.y3"))
                act.wait_ge(xcopy, 16)
                act.wait_ge(xout, l * (16 * TILES) + 1)
                act.dma_start(xf, out.rearrange("(t p) n -> p t n", p=P)).then_inc(xres_in, 16)
                act.wait_ge(kt_done, kt_value(l, IN_KTS - 1))
                for k in range(12):
                    y_hi(k)

                for t in back:
                    w = lambda st, s, t=t: act.wait_ge(st.sem, st.at(l, f"{t}.{s}"))
                    s = lambda step, t=t: (C_ACT.sem, C_ACT.one(f"{t}.{step}"))
                    n = t + 1

                    def probs(h):
                        for m in range(2):
                            b = Z["S"][h % 2][m][:, 0:P * n]
                            w(C_DVE, f"m{h}{m}")
                            nc.scalar.activation(b, b, ACT.Exp, bias=stat[:, 32 + 2 * h + m:33 + 2 * h + m],
                                                 accum_out=cden[:, 2 * h + m:2 * h + m + 1]).then_inc(*s(f"p{h}{m}"))

                    nc.scalar.activation(Z["GATE"], slot(SLOT["cz"])[:, t].rearrange("p (h c) -> p h c", h=HEADS),
                                         ACT.Exp, scale=-1.0).then_inc(*s("gate"))
                    for h in H:
                        probs(h)
                        w(C_PE, f"t{h}")
                        nc.scalar.activation(Z["WT"][h % 2][:, 0:n], mh[2][:, 0:n], ACT.Copy).then_inc(*s(f"wT{h}"))
                    w(C_DVE, "os")
                    nc.scalar.activation(Z["SQO"], Z["OS"], ACT.Square).then_inc(*s("sqo"))
                    w(C_DVE, "redo")
                    nc.scalar.activation(stat[:, 44:48], ss[:, 0:4], ACT.Ln, bias=eps_t[:, :], scale=1.0 / HD) \
                        .then_inc(*s("lno"))
                    w(C_ACT, "lno")
                    nc.scalar.activation(stat[:, 44:48], stat[:, 44:48], ACT.Exp, scale=-0.5).then_inc(*s("ro"))
                for k in range(12, 16):
                    y_hi(k)
                for n in T:
                    act.wait_ge(acc_free, acc_free_after(l, 18 + n, 3))
                    act.dma_start(out.rearrange("(t p) n -> p t n", p=P)[:, :, n * GW:n * GW + GW],
                                  xf[:, :, n * GW:n * GW + GW]).then_inc(xout, 16)
            act.wait_ge(xout, 16 * TILES * DEPTH + 1)

        @block.vector
        def _(dve):
            def plain():
                dve.sem_inc(dve_passed, 1)

            dve.memset(eps_t[:, :], EPS)
            dve.memset(smT[:, :], 1.0).then_inc(ones_done, 1)
            dve.wait_ge(params_in, 16 * (2 * DEPTH + 1))
            for l in range(DEPTH):
                for i in range(2):
                    a = slot(4)[:, l, PR["lam"] + 2 * DK * i:PR["lam"] + 2 * DK * i + DK]
                    b = slot(4)[:, l, PR["lam"] + 2 * DK * i + DK:PR["lam"] + 2 * DK * i + 2 * DK]
                    dve.scalar_tensor_tensor(general[:, 0, (2 * l + i) * DK:(2 * l + i + 1) * DK], a, 1.0, b, ALU.mult, ALU.mult,
                                             accum_out=stat[:, 2 * l + i:2 * l + i + 1]).then_inc(lam_steps, 1)
            dve.wait_ge(lam_act, 1)
            e = stat[:, 32:32 + 2 * DEPTH].rearrange("p (l i) -> p l i", i=2)
            dve.tensor_tensor(neg_lam[:, :], e[:, :, 1], e[:, :, 0], ALU.subtract).then_inc(lam_steps, 1)
            dve.wait_ge(lam_steps, 2 * DEPTH + 1)
            dve.tensor_tensor(neg_lam[:, :], neg_lam[:, :], slot(4)[:, 0:DEPTH, PR["linit"]], ALU.subtract) \
                .then_inc(lam_steps, 1)
            dve.tensor_scalar(pcol_all[:, :, PC["gq_b"]], pcol_all[:, :, PC["gq_b"]], HD ** -0.5, None, ALU.mult) \
                .then_inc(lam_steps, 1)
            dve.tensor_scalar(pcol_all[:, :, PC["gq_c"]], pcol_all[:, :, PC["gq_c"]], DK ** -0.5, None, ALU.mult) \
                .then_inc(lam_steps, 1)
            yc = pcol_all[:, :, PC["y"] + 12:PC["y"] + 16]
            dve.tensor_tensor(yc, yc, slot(4)[:, 0:DEPTH, PR["one_less"]:PR["one_less"] + 1]
                              .broadcast_to([P, DEPTH, 4]), ALU.mult).then_inc(lam_steps, 1)
            dve.wait_ge(lam_steps, 2 * DEPTH + 5)

            def gate(St, l, t, Zs, tmp):
                dve.wait_ge({id(D_DVE): D_ACT, id(A_DVE): A_ACT, id(B_DVE): B_ACT, id(C_DVE): C_ACT}[id(St)].sem,
                            {id(D_DVE): D_ACT, id(A_DVE): A_ACT, id(B_DVE): B_ACT, id(C_DVE): C_ACT}[id(St)]
                            .at(l, f"{t}.gate"))
                dve.tensor_scalar(tmp, tmp, 1.0, None, ALU.add).then_inc(St.sem, St.one(f"{t}.g1"))
                dve.wait_ge(St.sem, St.at(l, f"{t}.g1"))
                dve.reciprocal(tmp, tmp).then_inc(St.sem, St.one(f"{t}.g2"))
                dve.wait_ge(St.sem, St.at(l, f"{t}.g2"))
                dve.tensor_tensor(Zs, Zs, tmp, ALU.mult).then_inc(St.sem, St.one(f"{t}.g3"))

            with dve.Fori(0, DEPTH) as l:
                def sw(step):
                    dve.wait_ge(S_DVE.sem, S_DVE.at(l, step))

                def si(step):
                    return S_DVE.sem, S_DVE.one(step)

                dve.wait_ge(acc_free, l * (4 * N_ACC) + 4)
                dve.tensor_copy(pc[:, :], pcol_all[:, bass.ds(l, 1)].rearrange("p a n -> p (a n)")).then_inc(*si("pc"))
                dve.tensor_copy(pr[:, :], prow_all[:, bass.ds(l, 1)].rearrange("p a n -> p (a n)")).then_inc(*si("pr"))
                dve.tensor_copy(nlam[:, :], neg_lam[:, bass.ds(l, 1)]).then_inc(*si("lam"))
                dve.wait_ge(S_ACT.sem, S_ACT.at(l, "r"))
                dve.wait_ge(xout, l * (16 * TILES) + 1)
                for t in T:
                    dve.tensor_scalar(xf[:, t], xf[:, t], rs[:, t:t + 1], None, ALU.mult).then_inc(*si(f"x{t}"))
                for k in range(KT):
                    dve.wait_ge(S_ACT.sem, S_ACT.at(l, f"hi{k}"))
                    dve.scalar_tensor_tensor(actT_lo[:, k], mix[k % 4][:, :],
                                             pc[:, PC["norm"] + k:PC["norm"] + k + 1], actT_hi[:, k].bitcast(F32),
                                             ALU.mult, ALU.subtract).then_inc(*si(f"lo{k}"))

                def conv(c):
                    q = CHUNKS.index(c)
                    for b in range(4):
                        def ci(s):
                            return CONV_DVE.sem, CONV_DVE.one(f"{c}{b}{s}")

                        def cw(s):
                            dve.wait_ge(CONV_DVE.sem, CONV_DVE.at(l, f"{c}{b}{s}"))
                        src, dst = slot(SLOT[c])[:, b], slot(CONV[c])[:, b]
                        tap = [pc[:, PC["conv"] + 4 * (4 * q + b) + i:PC["conv"] + 4 * (4 * q + b) + i + 1]
                               for i in range(4)]
                        dve.wait_ge(acc_free, acc_free_after(l, q, b))
                        dve.tensor_scalar(dst, src, tap[3], None, ALU.mult).then_inc(*ci("t3"))
                        for i, prev in ((2, "t3"), (1, "t2"), (0, "t1")):
                            cw(prev)
                            d = 3 - i
                            dve.scalar_tensor_tensor(dst[:, d:], src[:, 0:SEQ - d], tap[i], dst[:, d:],
                                                     ALU.mult, ALU.add).then_inc(*ci(f"t{i}"))
                        dve.wait_ge(CONV_ACT.sem, CONV_ACT.at(l, f"{c}{b}"))
                        dve.tensor_scalar(general[:, b % 2], general[:, b % 2], 1.0, None, ALU.add) \
                            .then_inc(*ci("one"))
                        cw("one")
                        dve.reciprocal(general[:, b % 2], general[:, b % 2]).then_inc(*ci("rec"))
                        cw("rec")
                        dve.tensor_tensor(dst, dst, general[:, b % 2], ALU.mult).then_inc(*ci("mul"))

                dve.wait_ge(S_ACT.sem, S_ACT.at(l, "eb"))
                dve.tensor_scalar(beta[:, :, :], beta[:, :, :], 1.0, None, ALU.add).then_inc(*si("b1"))
                sw("b1")
                dve.reciprocal(beta[:, :, :], beta[:, :, :]).then_inc(*si("beta"))
                sw("beta")
                dve.tensor_scalar(nbeta[:, :, :], beta[:, :, :], -1.0, None, ALU.mult).then_inc(*si("nbeta"))
                av = small[:, :, HEADS:]
                dve.tensor_tensor(av, av, pr[:, PR["dtb"]:PR["dtb"] + 4].unsqueeze(1)
                                  .broadcast_to([P, TILES, HEADS]), ALU.add).then_inc(*si("av"))
                dve.wait_ge(S_ACT.sem, S_ACT.at(l, "A"))
                t16 = stat[:, 0:16].rearrange("p (t h) -> p t h", t=TILES)
                dve.scalar_tensor_tensor(glog[:, :, :], av, 0.0, t16, ALU.max, ALU.add).then_inc(*si("sp"))
                sw("sp")
                dve.tensor_scalar(glog[:, :, :], glog[:, :, :], -1.0, None, ALU.mult).then_inc(*si("glog"))
                sw("glog")
                dve.tensor_tensor(glog[:, :, :], glog[:, :, :], sa.unsqueeze(1).broadcast_to([P, TILES, HEADS]),
                                  ALU.mult).then_inc(*si("gA"))
                dve.wait_ge(masks_done, 2)
                conv("dq")
                conv("dk")
                conv("dv")
                dve.memset(U["S"][0], 0.0).then_inc(*si("zero_gdn"))

                for t in T:
                    w = lambda st, s, t=t: dve.wait_ge(st.sem, st.at(l, f"{t}.{s}"))
                    s = lambda step, t=t: (D_DVE.sem, D_DVE.one(f"{t}.{step}"))
                    b4, nb4 = beta[:, t], nbeta[:, t]
                    if t:
                        w2 = D_DVE.at(l, f"{t-1}.y3")
                        dve.wait_ge(D_DVE.sem, w2)
                    dve.tensor_tensor(U["AG"], heads(after), cols(glog[:, t]), ALU.mult).then_inc(*s("ag"))
                    w(D_ACT, "sqk")
                    dve.reduce_sum(ss[:, 0:8], U["SQ"], AX.X).then_inc(*s("red"))
                    w(D_ACT, "rr")
                    dve.tensor_tensor(U["QN"], mh[0], cols(rs[:, 0:4]), ALU.mult).then_inc(*s("qn"))
                    dve.tensor_tensor(U["KN"], mh[1], cols(rs[:, 4:8]), ALU.mult).then_inc(*s("kn"))
                    w(D_DVE, "qn")
                    dve.tensor_tensor(U["QD"], U["QN"], cols(decs[:, 0, t]), ALU.mult).then_inc(*s("qd"))
                    w(D_DVE, "kn")
                    dve.tensor_tensor(U["KB"], U["KN"], cols(decs[:, 0, t]), ALU.mult).then_inc(*s("kb"))
                    dve.tensor_tensor(U["KE"], U["KN"], cols(decs[:, 1, t]), ALU.mult).then_inc(*s("ke"))
                    w(D_ACT, "ex")
                    dve.tensor_tensor(U["EI"], U["EX"], heads(upto), ALU.mult).then_inc(*s("ei"))
                    w(D_DVE, "ei")
                    for h in H:
                        dve.scalar_tensor_tensor(U["EX"][:, h], U["EX"][:, h], nb4[:, h:h + 1], before,
                                                 ALU.mult, ALU.mult).then_inc(*s(f"es{h}"))
                    w(D_DVE, "es3")
                    w(D_PE, "kk")
                    dve.tensor_tensor(U["MT"], mh[0], U["EX"], ALU.mult).then_inc(*s("mt"))
                    w(D_PE, "kq")
                    dve.tensor_tensor(U["QK"], mh[1], U["EI"], ALU.mult).then_inc(*s("qk"))
                    dve.tensor_copy(U["X"], heads(ident)).then_inc(*s("xi"))
                    w(D_DVE, "xi")
                    w(D_PE, "m1")
                    plain()
                    dve.copy_predicated(U["X"], heads(m_x[0]), mh[2]).then_inc(*s("x1"))
                    for lv in range(2, LEVELS + 1):
                        w(D_PE, f"tx{lv}")
                        dve.tensor_copy(U["XT"], mh[1]).then_inc(*s(f"xt{lv}"))
                        if lv < LEVELS:
                            w(D_PE, f"p{lv}")
                            plain()
                            dve.copy_predicated(U["X"], heads(m_x[lv - 1]), mh[0]).then_inc(*s(f"x{lv}"))
                    w(D_DVE, "xt6")
                    w(D_PE, "pt6")
                    plain()
                    dve.copy_predicated(U["XT"], heads(m_xt6), mh[0]).then_inc(*s("xt7"))
                    gz = slot(SLOT["dz"])[:, t].rearrange("p (h c) -> p h c", h=HEADS)
                    gate(D_DVE, l, t, gz, U["GATE"])
                    w(D_PE, "u")
                    dve.tensor_tensor(U["UB"], mh[1], cols(b4), ALU.mult).then_inc(*s("ub"))
                    w(D_DVE, "ub")
                    for j in range(2):
                        r = slice(CH * j, CH * j + CH)
                        w(D_PE, f"v{j}")
                        for h in H:
                            dve.scalar_tensor_tensor(U["VW"][r, h], mh[3][r, h], b4[r, h:h + 1], U["UB"][r, h],
                                                     ALU.mult, ALU.add).then_inc(*s(f"v{j}{h}"))
                        w(D_PE, ("s0", "o")[j])
                        for h in H:
                            dve.scalar_tensor_tensor(U["S"][1 - j][:, h], U["S"][j][:, h],
                                                     decs[:, 2 + j, t, h:h + 1], mh[j][:, h],
                                                     ALU.mult, ALU.add).then_inc(*s(f"s{j}{h}"))
                    w(D_ACT, "sqo")
                    dve.reduce_sum(ss[:, 0:4], U["SQO"], AX.X).then_inc(*s("redo"))
                    w(D_ACT, "ro")
                    w(D_DVE, "g3")
                    for h in H:
                        dve.scalar_tensor_tensor(gz[:, h], mh[2][:, h], sa[:, h:h + 1], gz[:, h],
                                                 ALU.mult, ALU.mult).then_inc(*s(f"y{h}"))

                dve.wait_ge(D_DVE.sem, D_DVE.at(l, f"{TILES-1}.y3"))
                dve.memset(V["S"][:, 0], 0.0).then_inc(A_DVE.sem, A_DVE.one("zero_s"))
                dve.memset(V["AT"], 0.0).then_inc(A_DVE.sem, A_DVE.one("zero_a"))
                for t in T:
                    w = lambda st, s, t=t: dve.wait_ge(st.sem, st.at(l, f"{t}.{s}"))
                    s = lambda step, t=t: (A_DVE.sem, A_DVE.one(f"{t}.{step}"))
                    q, k = slot(SLOT["aq"])[:, t, 0:256], slot(SLOT["aq"])[:, t, 256:512]
                    w(A_ACT, "l")
                    dve.scalar_tensor_tensor(V["G"], mix[1][:, 0:256], 0.0, V["T0"], ALU.min, ALU.subtract) \
                        .then_inc(*s("g"))
                    w(A_ACT, "er")
                    if t == 0:
                        dve.wait_ge(acc_free, acc_free_after(l, CHUNKS.index("av"), 3))
                    dve.scalar_tensor_tensor(V["QD"], V["EB"], DK ** -0.5, q, ALU.mult, ALU.mult).then_inc(*s("qd"))
                    dve.tensor_tensor(V["KI"], V["ENB"], k, ALU.mult).then_inc(*s("ki"))
                    dve.tensor_tensor(V["KE"], V["ER"], k, ALU.mult).then_inc(*s("ke"))
                    w(A_PE, "a")
                    w(A_DVE, "ke")
                    for i in range(2):
                        plain()
                        dve.copy_predicated(V["AT"][:, i::2], heads(m_upto)[:, 0:2], mh[3 - i][:, i::2]) \
                            .then_inc(*s(f"at{i}"))
                    w(A_PE, "us")
                    w(A_ACT, "dect")
                    w(A_DVE, "at1")
                    for j in range(2):
                        if j:
                            w(A_DVE, "s01")
                        for p in range(2):
                            dve.scalar_tensor_tensor(V["S"][:, (2 * t + j + 1) % 3, p], V["S"][:, (2 * t + j) % 3, p],
                                                     V["DECT"][:, 2 * p + j:2 * p + j + 1], mh[j][:, p],
                                                     ALU.mult, ALU.add).then_inc(*s(f"s{j}{p}"))
                    gz = slot(SLOT["az"])[:, t].rearrange("p (h c) -> p h c", h=HEADS)
                    gate(A_DVE, l, t, gz, V["GATE"])
                    w(A_ACT, "sqo1")
                    dve.reduce_sum(ss[:, 0:4], V["SQO"], AX.X).then_inc(*s("redo"))
                    w(A_ACT, "ro")
                    w(A_DVE, "g3")
                    for h in H:
                        dve.scalar_tensor_tensor(gz[:, h], mh[3 if h % 2 else 1][:, h], sa[:, h:h + 1], gz[:, h],
                                                 ALU.mult, ALU.mult).then_inc(*s(f"y{h}"))

                def sums(t):
                    s = lambda step: (N_DVE.sem, N_DVE.one(f"{t}.{step}"))
                    dve.wait_ge(N_ACT.sem, N_ACT.at(l, f"{t}.bk"))
                    dve.reduce_sum(ssb, W["SQ"], AX.X).then_inc(*s("redb"))
                    dve.wait_ge(N_ACT.sem, N_ACT.at(l, f"{t}.ck"))
                    dve.reduce_sum(ss, RQ, AX.X).then_inc(*s("redc"))

                def normalise(t):
                    s = lambda step: (N_DVE.sem, N_DVE.one(f"{t}.{step}"))
                    q = slot(SLOT["bq"])[:, t].rearrange("p (h c) -> p h c", h=HEADS)
                    k = slot(SLOT["bkv"])[:, t, 0:256].rearrange("p (h c) -> p h c", h=2)
                    dve.wait_ge(N_ACT.sem, N_ACT.at(l, f"{t}.rb"))
                    dve.tensor_tensor(q, q, cols(rsb[:, 0:4]), ALU.mult).then_inc(*s("bq"))
                    dve.tensor_tensor(k, k, cols(rsb[:, 4:6]), ALU.mult).then_inc(*s("bk"))
                    dve.wait_ge(N_ACT.sem, N_ACT.at(l, f"{t}.rc"))
                    for i, c in enumerate("qk"):
                        v = slot(SLOT["c" + c])[:, t].rearrange("p (g c) -> p g c", c=DK)
                        dve.tensor_tensor(v, v, cols(rs[:, 8 * i:8 * i + 8], n=DK), ALU.mult).then_inc(*s("c" + c))

                sums(0)
                normalise(0)
                for t in T:
                    w = lambda st, s, t=t: dve.wait_ge(st.sem, st.at(l, f"{t}.{s}"))
                    s = lambda step, t=t: (B_DVE.sem, B_DVE.one(f"{t}.{step}"))
                    n = P * (min(t, 1) + 1)
                    for h in H:
                        w(B_PE, f"s{h//2}")
                        dve.scalar_tensor_tensor(W["SB"][:, h, 0:n], win[:, 256 - n:256], -SLOPES_B[h],
                                                 mix[2 + h // 2][:, 256 * (h % 2):256 * (h % 2) + n],
                                                 ALU.mult, ALU.add).then_inc(*s(f"b{h}"))
                    w(B_DVE, "b3")
                    dve.reduce_max(sa, W["SB"][:, :, 0:n], AX.X).then_inc(*s("mx"))
                    w(B_DVE, "mx")
                    dve.tensor_tensor(sa, sa, pr[:, PR["sink"]:PR["sink"] + 4], ALU.max).then_inc(*s("mxs"))
                    w(B_DVE, "mxs")
                    dve.tensor_scalar(sb2, sa, -1.0, None, ALU.mult).then_inc(*s("nm"))
                    w(B_DVE, "nm")
                    dve.tensor_tensor(sd, sb2, pr[:, PR["sink"]:PR["sink"] + 4], ALU.add).then_inc(*s("es"))
                    if t + 1 < TILES:
                        sums(t + 1)
                    gz = slot(SLOT["bz"])[:, t].rearrange("p (h c) -> p h c", h=HEADS)
                    gate(B_DVE, l, t, gz, W["GATE"])
                    w(B_ACT, "es")
                    dve.tensor_tensor(se, sc, sd, ALU.add).then_inc(*s("den"))
                    w(B_DVE, "den")
                    dve.reciprocal(se, se).then_inc(*s("rd"))
                    if t + 1 < TILES:
                        normalise(t + 1)
                    w(B_PE, "pt1")
                    dve.tensor_copy(W["PT"][:, 2:4, 0:n],
                                    mix[1][:, :].rearrange("p (h c) -> p h c", h=2)[:, :, 0:n]).then_inc(*s("PT1"))
                    w(B_PE, "pv")
                    w(B_DVE, "g3")
                    for h in H:
                        dve.scalar_tensor_tensor(gz[:, h], mh[2][:, h], se[:, h:h + 1], gz[:, h],
                                                 ALU.mult, ALU.mult).then_inc(*s(f"y{h}"))

                def y_lo(k):
                    dve.wait_ge(S_ACT.sem, S_ACT.at(l, f"yhi{k}"))
                    dve.scalar_tensor_tensor(actT_lo[:, k], mix[k % 4][:, :], pc[:, PC["y"] + k:PC["y"] + k + 1],
                                             actT_hi[:, k].bitcast(F32), ALU.mult, ALU.subtract) \
                        .then_inc(*si(f"ylo{k}"))

                def add(q, n, last_kt):
                    for b in range(4):
                        wait_acc(dve, l, q, b, last_kt)
                        xs = xf[:, b, n * GW:n * GW + GW]
                        dve.tensor_tensor(xs, acc[b][:, :], xs, ALU.add).then_inc(acc_free, 1)

                for k in range(12):
                    y_lo(k)
                for t in back:
                    w = lambda st, s, t=t: dve.wait_ge(st.sem, st.at(l, f"{t}.{s}"))
                    s = lambda step, t=t: (C_DVE.sem, C_DVE.one(f"{t}.{step}"))
                    n = P * (t + 1)
                    for h in H:
                        S = Z["S"][h % 2]
                        w(C_PE, f"s{h}")
                        if h >= 2:
                            w(C_PE, f"t{h-2}")
                        for m in range(2):
                            dve.scalar_tensor_tensor(S[m][:, 0:n], dist[:, 384 - P * t:384 - P * t + n], -SLOPES_C[h],
                                                     mix[m][:, 0:n], ALU.mult, ALU.add).then_inc(*s(f"b{h}{m}"))
                        for m in range(2):
                            w(C_DVE, f"b{h}{m}")
                            dve.tensor_reduce(stat[:, 32 + 2 * h + m:33 + 2 * h + m], S[m][:, 0:n], AX.X, ALU.max,
                                              negate=True).then_inc(*s(f"m{h}{m}"))
                        w(C_ACT, f"p{h}1")
                        dve.reciprocal(stat[:, 16 + 2 * h:18 + 2 * h], cden[:, 2 * h:2 * h + 2]) \
                            .then_inc(*s(f"r{h}"))
                        w(C_DVE, f"r{h}")
                        dve.scalar_tensor_tensor(stat[:, 24 + h:25 + h], stat[:, 17 + 2 * h:18 + 2 * h],
                                                 cden[:, 2 * h:2 * h + 1], nlam[:, :], ALU.mult, ALU.mult) \
                            .then_inc(*s(f"c{h}"))
                        w(C_DVE, f"c{h}")
                        dve.scalar_tensor_tensor(S[0][:, 0:n], S[1][:, 0:n], stat[:, 24 + h:25 + h], S[0][:, 0:n],
                                                 ALU.mult, ALU.add).then_inc(*s(f"w{h}"))
                    gz = slot(SLOT["cz"])[:, t].rearrange("p (h c) -> p h c", h=HEADS)
                    gate(C_DVE, l, t, gz, Z["GATE"])
                    if t == TILES - 1:
                        dve.wait_ge(xres_in, l * 16 + 16)
                        add(14, 0, IN_KTS + 11)
                    w(C_PE, "v3")
                    dve.tensor_tensor(Z["OS"], mh[3], cols(stat[:, 16:24:2]), ALU.mult).then_inc(*s("os"))
                    w(C_ACT, "sqo")
                    dve.reduce_sum(ss[:, 0:4], Z["SQO"], AX.X).then_inc(*s("redo"))
                    w(C_ACT, "ro")
                    w(C_DVE, "g3")
                    for h in H:
                        dve.scalar_tensor_tensor(gz[:, h], Z["OS"][:, h], stat[:, 44 + h:45 + h], gz[:, h],
                                                 ALU.mult, ALU.mult).then_inc(*s(f"y{h}"))
                    if t < TILES - 1:
                        add(14 + TILES - 1 - t, TILES - 1 - t, IN_KTS + 12 * (TILES - t) - 1)
                for k in range(12, 16):
                    y_lo(k)
                for n in T:
                    add(18 + n, n, IN_KTS + OUT_KTS + 4 * n + 3)


def constants():
    s, c = np.arange(P)[:, None], np.arange(P)[None, :]
    same = (s // CH) == (c // CH)
    f = [s == c, same & (s <= c), same & (s > c), same & (s < c), (s < CH) & (c >= 0), (s >= CH) & (c >= 0)]
    f = [a.astype(np.float32) for a in f]
    d = s + P - np.arange(2 * P)[None, :]
    f.append(np.where((d >= 0) & (d < P), d, BIG).astype(np.float32))
    d = s + 3 * P - np.arange(7 * P)[None, :]
    f.append(np.where(d >= 0, d, BIG).astype(np.float32))
    u = []
    for lv in range(LEVELS):
        b = 2 ** lv
        low = ((s // (2 * b)) == (c // (2 * b))) & ((s // b) % 2 == 1) & ((c // b) % 2 == 0)
        u.append(low)
    u = [a.astype(np.float32) for a in u]
    u[-1] = np.ascontiguousarray(u[-1].T)
    return np.concatenate(f, 1), np.concatenate(u, 1)


def kernel(**inputs):
    import concourse.bacc as bacc
    from concourse.bass_utils import run_bass_kernel_spmd

    a = {k: np.asarray(v) for k, v in inputs.items()}
    L = DEPTH
    win = a["w_in"].reshape(L, KT, P, -1)
    parts = [win[..., OFF[c]:OFF[c] + GW] for c in CHUNKS]
    wo = a["w_out"].reshape(L, 4, HEADS, P, D_MODEL)[:, OUT_GROUPS].reshape(L, KT, P, D_MODEL)
    parts += [wo[:, 0:12, :, n * GW:n * GW + GW] for n in range(TILES)]
    parts += [wo[:, 12:16, :, n * GW:n * GW + GW] for n in range(TILES)]
    ws = np.concatenate(parts, 1).reshape(L, PAIRS, 2, P, GW).transpose(0, 1, 3, 2, 4)
    wstream = np.ascontiguousarray(ws).reshape(L * PAIRS, P, 2 * GW)
    sm = np.concatenate([win[..., OFF["alr"]:OFF["alr"] + RANK], win[..., OFF["dbeta"]:OFF["dbeta"] + 2 * HEADS]], -1)
    wsmall = np.ascontiguousarray(sm.transpose(0, 2, 1, 3)).reshape(L, P, KT * NSM)
    pcol = np.zeros((L, P, NPC), np.float32)
    pcol[:, :, 0:KT] = a["norm_g"].reshape(L, KT, P).transpose(0, 2, 1)
    pcol[:, :, 16:20] = a["gdn_norm_g"][:, :, None]
    pcol[:, :, 20:24] = a["gla_norm_g"][:, :, None]
    pcol[:, :, 24:28] = 1.0
    pcol[:, :, 28:32] = a["diff_subln_g"][:, :, None]
    pcol[:, :, PC["gq_b"]] = a["swa_q_norm_g"]
    pcol[:, :, PC["gk_b"]] = a["swa_k_norm_g"]
    for i in range(2):
        pcol[:, DK * i:DK * i + DK, PC["gq_c"]] = a["diff_q_norm_g"]
        pcol[:, DK * i:DK * i + DK, PC["gk_c"]] = a["diff_k_norm_g"]
    pcol[:, :, PC["conv"]:] = a["gdn_conv_w"].reshape(L, 4, 12, P).transpose(0, 3, 2, 1).reshape(L, P, 48)
    prow = np.zeros((L, NPR), np.float32)
    prow[:, 0:4] = a["swa_sinks"]
    prow[:, 4:8] = a["gdn_A_log"]
    prow[:, 8:12] = a["gdn_dt_bias"]
    prow[:, 12:12 + 4 * DK] = a["diff_lambda"].reshape(L, 4 * DK)
    init = [0.8 - 0.6 * math.exp(-0.3 * l) for l in range(L)]
    prow[:, PR["linit"]] = init
    prow[:, PR["one_less"]] = [1.0 - i for i in init]
    wlr = np.concatenate([a["gla_w_lr2"], np.zeros((L, 2 * HEADS, HEADS * DK), np.float32),
                          a["gla_b_lr2"][:, None, :]], 1)
    cf, masks = constants()
    arrays = dict(x=a["x"].reshape(SEQ, D_MODEL), wstream=wstream, wsmall=wsmall, pcol=pcol, prow=prow,
                  wlr=wlr, cf=cf, masks=masks)
    arrays = {f"in_{k}": np.ascontiguousarray(v) for k, v in arrays.items()}

    nc = bacc.Bacc("TRN2", target_bir_lowering=False, num_devices=1)
    args = [nc.dram_tensor(k, v.shape, mybir.dt.from_np(v.dtype), kind="ExternalInput").ap()
            for k, v in arrays.items()]
    args.append(nc.dram_tensor("out_x", (SEQ, D_MODEL), F32, kind="ExternalOutput").ap())
    hybrid_trunk(nc, *args)
    r = run_bass_kernel_spmd(nc, [arrays], core_ids=[0])
    return r.results[0]["out_x"].reshape(1, SEQ, D_MODEL)
```
